# Optimizing a Trainium2 kernel written in Bass

```python
import jax, jax.numpy as jnp
from jax import lax
import numpy as np

D_MODEL = 1024
BATCH = 1
SEQ = 512
DEPTH = 1
DEC_BATCH = 1
DEC_SEQ = 64
PAST_LEN = 1024

CHUNK = 64
D_MIX = D_MODEL
D_POOL = D_MIX // 2
POOL_WINDOWS = (2, 4, 8, 16)
N_POOL_GROUPS = len(POOL_WINDOWS)
POOL_GROUP_W = D_POOL // N_POOL_GROUPS
POOL_HIST = max(POOL_WINDOWS) - 1
D_FOX = D_MIX - D_POOL
FOX_HEADS = 8
FOX_HEAD_DIM = D_FOX // FOX_HEADS
Q_BLOCK = 128
N_MEM = 256
MEM_HEADS = 4
MEM_HEAD_DIM = D_MODEL // MEM_HEADS
D_FF = ((8 * D_MODEL // 3 + 127) // 128) * 128
CONV_W = 3
D_IN = D_POOL + 3 * D_FOX + FOX_HEADS
FORGET_BIAS = 3.0
EPS = 1e-6

kernel_name = 'hybrid_pool_fox_stream_encoder_step'

def rmsnorm(x, g):
    x32 = x.astype(jnp.float32)
    y = x32 * lax.rsqrt(jnp.mean(x32 * x32, axis=-1, keepdims=True) + EPS)
    return (y * g.astype(jnp.float32)).astype(x.dtype)

def pool_mixer(u, u_hist, pos0, w_pool, pool_scale):
    B, T, _ = u.shape
    nh = u_hist.shape[1]
    u_ext = jnp.concatenate([u_hist.astype(u.dtype), u], axis=1).astype(jnp.float32)
    cs = jnp.cumsum(u_ext, axis=1)
    cs = jnp.concatenate([jnp.zeros((B, 1, D_POOL), jnp.float32), cs], axis=1)
    upper = cs[:, nh + 1:]
    t_idx = jnp.arange(T)
    diffs = []
    for g, w in enumerate(POOL_WINDOWS):
        sl = slice(g * POOL_GROUP_W, (g + 1) * POOL_GROUP_W)
        lo = jnp.maximum(t_idx + nh + 1 - w, 0)
        lower = jnp.take(cs[:, :, sl], lo, axis=1)
        count = jnp.minimum(pos0 + t_idx + 1, w).astype(jnp.float32)
        mean = (upper[:, :, sl] - lower) / count[None, :, None]
        diffs.append(mean - u_ext[:, nh:, sl])
    d = jnp.stack(diffs, axis=2).astype(u.dtype)
    y = jnp.einsum('btgc,gcd->btgd', d, w_pool).reshape(B, T, D_POOL)
    return y * pool_scale

def fox_attention(q, k, v, cq, ck, q_pos, k_pos):
    B, Tq, H, Dh = q.shape
    qb = Q_BLOCK if Tq % Q_BLOCK == 0 else Tq
    nb = Tq // qb
    scale = FOX_HEAD_DIM ** -0.5
    q_blocks = q.reshape(B, nb, qb, H, Dh).transpose(1, 0, 2, 3, 4)
    cq_blocks = cq.reshape(B, nb, qb, H).transpose(1, 0, 3, 2)
    pos_blocks = q_pos.reshape(nb, qb)
    ck_t = ck.transpose(0, 2, 1)

    def one_block(args):
        qblk, cblk, pblk = args
        s = jnp.einsum('bqhd,bkhd->bhqk', qblk, k).astype(jnp.float32) * scale
        s = s + (cblk[:, :, :, None] - ck_t[:, :, None, :])
        causal = pblk[:, None] >= k_pos[None, :]
        s = jnp.where(causal[None, None], s, -jnp.inf)
        p = jax.nn.softmax(s, axis=-1)
        return jnp.einsum('bhqk,bkhd->bqhd', p.astype(v.dtype), v)

    out = lax.map(one_block, (q_blocks, cq_blocks, pos_blocks))
    return out.transpose(1, 0, 2, 3, 4).reshape(B, Tq, H, Dh)

def memory_kv(mem, g_mkv, w_mk, w_mv):
    B, M, _ = mem.shape
    m = rmsnorm(mem, g_mkv)
    mk = (m @ w_mk).reshape(B, M, MEM_HEADS, MEM_HEAD_DIM)
    mv = (m @ w_mv).reshape(B, M, MEM_HEADS, MEM_HEAD_DIM)
    return mk, mv

def encoder_layer(x, k_hist, v_hist, logf_hist, pool_hist, conv_hist, mem_k, mem_v, pos0,
                  g_mix, w_in, b_f, w_pool, pool_scale, w_o, g_xq, w_mq, w_mo,
                  g_ffn, w_up, conv_w, conv_b, w_down):
    B, T, _ = x.shape
    h = rmsnorm(x, g_mix)
    z = h @ w_in
    u = z[..., :D_POOL]
    q = z[..., D_POOL:D_POOL + D_FOX].reshape(B, T, FOX_HEADS, FOX_HEAD_DIM)
    k = z[..., D_POOL + D_FOX:D_POOL + 2 * D_FOX].reshape(B, T, FOX_HEADS, FOX_HEAD_DIM)
    v = z[..., D_POOL + 2 * D_FOX:D_POOL + 3 * D_FOX].reshape(B, T, FOX_HEADS, FOX_HEAD_DIM)
    logf = jax.nn.log_sigmoid((z[..., D_POOL + 3 * D_FOX:] + b_f).astype(jnp.float32))

    nh = k_hist.shape[1]
    k_all = jnp.concatenate([k_hist.astype(k.dtype), k], axis=1)
    v_all = jnp.concatenate([v_hist.astype(v.dtype), v], axis=1)
    c_all = jnp.cumsum(jnp.concatenate([logf_hist.astype(jnp.float32), logf], axis=1), axis=1)
    q_pos = pos0 + jnp.arange(T)
    k_pos = jnp.arange(nh + T) + (pos0 - nh)
    o_fox = fox_attention(q, k_all, v_all, c_all[:, nh:], c_all, q_pos, k_pos).reshape(B, T, D_FOX)

    o_pool = pool_mixer(u, pool_hist, pos0, w_pool, pool_scale)
    x = x + jnp.concatenate([o_pool.astype(x.dtype), o_fox.astype(x.dtype)], axis=-1) @ w_o

    mq = (rmsnorm(x, g_xq) @ w_mq).reshape(B, T, MEM_HEADS, MEM_HEAD_DIM)
    s = jnp.einsum('bthd,bmhd->bhtm', mq, mem_k.astype(mq.dtype)).astype(jnp.float32) * (MEM_HEAD_DIM ** -0.5)
    p = jax.nn.softmax(s, axis=-1)
    mo = jnp.einsum('bhtm,bmhd->bthd', p.astype(x.dtype), mem_v.astype(x.dtype)).reshape(B, T, D_MODEL)
    x = x + mo @ w_mo

    up = rmsnorm(x, g_ffn) @ w_up
    a, b = up[..., :D_FF], up[..., D_FF:]
    a_ext = jnp.concatenate([conv_hist.astype(a.dtype), a], axis=1)
    conv = conv_b + sum(a_ext[:, j:j + T] * conv_w[j] for j in range(CONV_W))
    x = x + (jax.nn.silu(conv) * b) @ w_down

    pool_new = jnp.concatenate([pool_hist.astype(u.dtype), u], axis=1)[:, -POOL_HIST:]
    conv_new = a_ext[:, -(CONV_W - 1):]
    return x, (k, v, logf, pool_new, conv_new)

def setup_inputs(seed: int = 0) -> dict:
    key = jax.random.key(seed)
    ks = jax.random.split(key, 32)
    f32 = jnp.float32
    nrm = lambda k, shape, s: jax.random.normal(k, shape, f32) * s
    inp = {
        'x_prompt': nrm(ks[0], (BATCH, SEQ, D_MODEL), 1.0),
        'x_sample': nrm(ks[1], (DEC_BATCH, DEC_SEQ, D_MODEL), 1.0),
        'cache_fox_k': nrm(ks[2], (DEPTH, DEC_BATCH, PAST_LEN, FOX_HEADS, FOX_HEAD_DIM), 1.0),
        'cache_fox_v': nrm(ks[3], (DEPTH, DEC_BATCH, PAST_LEN, FOX_HEADS, FOX_HEAD_DIM), 1.0),
        'cache_fox_logf': jax.nn.log_sigmoid(FORGET_BIAS + nrm(ks[4], (DEPTH, DEC_BATCH, PAST_LEN, FOX_HEADS), 1.0)),
        'state_pool': nrm(ks[5], (DEPTH, DEC_BATCH, POOL_HIST, D_POOL), 1.0),
        'state_ffn_conv': nrm(ks[6], (DEPTH, DEC_BATCH, CONV_W - 1, D_FF), 1.0),
        'cache_mem_k': nrm(ks[7], (DEPTH, DEC_BATCH, N_MEM, MEM_HEADS, MEM_HEAD_DIM), 1.0),
        'cache_mem_v': nrm(ks[8], (DEPTH, DEC_BATCH, N_MEM, MEM_HEADS, MEM_HEAD_DIM), 1.0),
        'mem_prompt': nrm(ks[9], (BATCH, N_MEM, D_MODEL), 1.0),
        'g_mix': 1.0 + nrm(ks[10], (DEPTH, D_MODEL), 0.05),
        'w_in': nrm(ks[11], (DEPTH, D_MODEL, D_IN), D_MODEL ** -0.5),
        'b_f': FORGET_BIAS + nrm(ks[12], (DEPTH, FOX_HEADS), 0.5),
        'w_pool': nrm(ks[13], (DEPTH, N_POOL_GROUPS, POOL_GROUP_W, POOL_GROUP_W), POOL_GROUP_W ** -0.5),
        'pool_scale': 1.0 + nrm(ks[14], (DEPTH, D_POOL), 0.1),
        'w_o': nrm(ks[15], (DEPTH, D_MIX, D_MODEL), D_MIX ** -0.5),
        'g_xq': 1.0 + nrm(ks[16], (DEPTH, D_MODEL), 0.05),
        'g_mkv': 1.0 + nrm(ks[17], (DEPTH, D_MODEL), 0.05),
        'w_mq': nrm(ks[18], (DEPTH, D_MODEL, D_MODEL), D_MODEL ** -0.5),
        'w_mk': nrm(ks[19], (DEPTH, D_MODEL, D_MODEL), D_MODEL ** -0.5),
        'w_mv': nrm(ks[20], (DEPTH, D_MODEL, D_MODEL), D_MODEL ** -0.5),
        'w_mo': nrm(ks[21], (DEPTH, D_MODEL, D_MODEL), D_MODEL ** -0.5),
        'g_ffn': 1.0 + nrm(ks[22], (DEPTH, D_MODEL), 0.05),
        'w_up': nrm(ks[23], (DEPTH, D_MODEL, 2 * D_FF), D_MODEL ** -0.5),
        'conv_w': nrm(ks[24], (DEPTH, CONV_W, D_FF), CONV_W ** -0.5),
        'conv_b': nrm(ks[25], (DEPTH, D_FF), 0.01),
        'w_down': nrm(ks[26], (DEPTH, D_FF, D_MODEL), D_FF ** -0.5),
        'g_final': 1.0 + nrm(ks[27], (D_MODEL,), 0.05),
    }
    return inp

def reference(x_prompt, x_sample, cache_fox_k, cache_fox_v, cache_fox_logf, state_pool, state_ffn_conv,
              cache_mem_k, cache_mem_v, mem_prompt, g_mix, w_in, b_f, w_pool, pool_scale, w_o,
              g_xq, g_mkv, w_mq, w_mk, w_mv, w_mo, g_ffn, w_up, conv_w, conv_b, w_down, g_final):
    xp, xs = x_prompt, x_sample
    bp = xp.shape[0]
    past = cache_fox_k.shape[2]
    pk, pv, plf, ppool, pconv, pmk, pmv = [], [], [], [], [], [], []
    sk, sv, slf, spool, sconv = [], [], [], [], []
    for l in range(DEPTH):
        lw = (g_mix[l], w_in[l], b_f[l], w_pool[l], pool_scale[l], w_o[l], g_xq[l], w_mq[l], w_mo[l],
              g_ffn[l], w_up[l], conv_w[l], conv_b[l], w_down[l])
        mk, mv = memory_kv(mem_prompt, g_mkv[l], w_mk[l], w_mv[l])
        xp, st_p = encoder_layer(
            xp,
            jnp.zeros((bp, 0, FOX_HEADS, FOX_HEAD_DIM), xp.dtype),
            jnp.zeros((bp, 0, FOX_HEADS, FOX_HEAD_DIM), xp.dtype),
            jnp.zeros((bp, 0, FOX_HEADS), jnp.float32),
            jnp.zeros((bp, 0, D_POOL), xp.dtype),
            jnp.zeros((bp, CONV_W - 1, D_FF), xp.dtype),
            mk, mv, 0, *lw)
        xs, st_s = encoder_layer(
            xs, cache_fox_k[l], cache_fox_v[l], cache_fox_logf[l], state_pool[l], state_ffn_conv[l],
            cache_mem_k[l], cache_mem_v[l], past, *lw)
        pk.append(st_p[0]); pv.append(st_p[1]); plf.append(st_p[2]); ppool.append(st_p[3]); pconv.append(st_p[4])
        pmk.append(mk); pmv.append(mv)
        sk.append(st_s[0]); sv.append(st_s[1]); slf.append(st_s[2]); spool.append(st_s[3]); sconv.append(st_s[4])
    y_prompt = rmsnorm(xp, g_final)
    y_sample = rmsnorm(xs, g_final)
    return (y_prompt, y_sample,
            jnp.stack(pk), jnp.stack(pv), jnp.stack(plf), jnp.stack(ppool), jnp.stack(pconv),
            jnp.stack(pmk), jnp.stack(pmv),
            jnp.stack(sk), jnp.stack(sv), jnp.stack(slf), jnp.stack(spool), jnp.stack(sconv))


_drawn_inputs = setup_inputs


def setup_inputs(seed=0):
    import zlib

    import numpy as np

    out = dict(_drawn_inputs(seed))
    spreads = {}
    factors = {'cache_fox_logf': 3.535, 'g_xq': 8.0, 'conv_b': 8.0}
    for name, (base, spread) in spreads.items():
        noise = np.random.default_rng([zlib.crc32(name.encode()), seed]).standard_normal(out[name].shape)
        drawn = base * np.exp(spread * noise) if base else spread * noise
        out[name] = __import__('jax').numpy.asarray(drawn.astype(out[name].dtype))
    for name, factor in factors.items():
        out[name] = (out[name] * factor).astype(out[name].dtype)
    return out
```

```python
from contextlib import ExitStack

import concourse.bass as bass
from concourse import mybir
from concourse.alu_op_type import AluOpType as ALU

ACT = mybir.ActivationFunctionType
F32 = mybir.dt.float32
F32R = mybir.dt.float32r
X = mybir.AxisListType.X
P = 128
EPS = 1e-6
MASKED = -1e30
DMA_SCRATCH = 3072


class Tally:

    def __init__(self, sem):
        self.sem, self.base, self.n, self.i, self.per = sem, 0, 0, None, 0

    @property
    def now(self):
        return self.base + self.n if self.i is None else self.i * self.per + (self.base + self.n)

    def inc(self, instruction):
        instruction.then_inc(self.sem, 1)
        self.n += 1

    def enter(self, i, per):
        self.base, self.n, self.i, self.per = self.base + self.n, 0, i, per

    def leave(self, rounds):
        assert self.n == self.per, (self.n, self.per)
        self.base, self.n, self.i = self.base + rounds * self.per, 0, None


def build(nc, a, o):
    TP, D = a["x_prompt"].shape[1:]
    TS = a["x_sample"].shape[1]
    T = TP + TS
    H = T // 2
    KT = D // P
    PAST, HEADS, DH = a["cache_fox_k"].shape[2:]
    DFOX = HEADS * DH
    PAIRS = HEADS // 2
    NHIST, DPOOL = a["state_pool"].shape[2:]
    GROUPS = DPOOL // P
    DFF = a["w_down"].shape[1]
    NF = DFF // P
    MEM, MH, MD = a["cache_mem_k"].shape[2:]
    MT = MEM // P
    NT = TP // P
    CT = PAST // P
    KEYS = PAST + TS
    QSCALE = float(DH) ** -0.5
    MSCALE = float(MD) ** -0.5
    D_IN = DPOOL + 3 * DFOX + HEADS
    assert 2 * DH == P and MD == 2 * P and TS == DH and KT == 8 and NT == 4 and MT == 2

    CHUNKS = [(0, 8), (8, 8), (16, 6)]
    assert sum(c[1] for c in CHUNKS) == NF
    W_V, W_QK, W_U, W_O, W_MK, W_MQ, W_MV, W_MO = 0, 4, 12, 16, 24, 32, 40, 48
    A_QK, A_U, A_POOL, A_O, A_MQ, A_MO = 0, 8, 12, 16, 24, 32
    W_UP, W_DOWN, A_UP, A_DOWN = [], [], [], []
    w_all, a_all = 56, 40
    for _, nf in CHUNKS:
        W_UP.append(w_all)
        W_DOWN.append(w_all + 2 * nf)
        A_UP.append(a_all)
        A_DOWN.append(a_all + 2 * nf)
        w_all += 2 * nf + KT
        a_all += 2 * nf + KT

    ENTRIES, LAG = 2 * NT + 3, 3
    N_ENTRIES = PAIRS * ENTRIES
    TURNS = []
    for s in range(N_ENTRIES + LAG):
        j, e = divmod(s, ENTRIES)
        if j < PAIRS and e in (2, 5):
            TURNS.append(("K", j, 0 if e == 2 else 1))
        if s >= LAG:
            TURNS.append(("P", s - LAG))
    TURN = {what: n for n, what in enumerate(TURNS)}
    FILL = {0: (0, [0, 1]), 1: (0, [2, 3]), 2: (0, [4, 5]), 3: (0, [6]), 4: (0, [7]),
            5: (1, [0, 1]), 6: (1, [2, 3]), 7: (1, [4, 5]), 8: (1, [6]), 9: (1, [7])}

    decay_p_dram = nc.dram_tensor("decay_prompt", (HEADS, TP), F32, kind="Internal").ap()
    decay_s_dram = nc.dram_tensor("decay_sample", (HEADS, KEYS), F32, kind="Internal").ap()

    ctx = ExitStack()
    with ctx:
        slab_bytes = (nc.sbuf_bytes_remaining - 96) // 32 * 32
        slab_at = (nc.sbuf_base + 31) // 32 * 32
        ctx.enter_context(nc.sbuf_tensor("slab", [P, slab_bytes // 4], F32))
        at = {}
        here = [0]

        def place(name, shape, dtype=F32):
            size = 4
            for s in shape[1:]:
                size *= s
            at[name] = here[0]
            here[0] += (size + 31) // 32 * 32
            assert here[0] <= slab_bytes, (name, here[0], slab_bytes)
            return nc.alloc_sbuf_tensor_at(name, shape, dtype, offset=slab_at + at[name])

        w_raw = [place(f"w_raw{s}", [P, D]) for s in range(2)]
        w_hi = [place(f"w_hi{s}", [P, D], F32R) for s in range(2)]
        w_lo = [place(f"w_lo{s}", [P, D], F32R) for s in range(2)]
        flat_a = [place(f"a_{s}", [P, KT * T + P - TS], F32R) for s in ("hi", "lo")]
        a_hi, a_lo = (x[:, 0:KT * T].rearrange("p (k t) -> p k t", k=KT) for x in flat_a)
        flat_b = [place(f"b_{s}", [P, KT * T + P - TS], F32R) for s in ("hi", "lo")]
        b_hi, b_lo = (x[:, 0:KT * T].rearrange("p (k t) -> p k t", k=KT) for x in flat_b)
        ident = place("ident", [P, P])
        ident_r = place("ident_r", [P, P], F32R)
        causal_r = place("causal_r", [P, P], F32R)
        causal_s = place("causal_s", [P, DH], F32R)
        mean_w = place("mean_w", [P, P])
        eps = place("eps", [P, 1])
        one = place("one", [P, 1])
        NG = 4 * KT + GROUPS
        gains = place("gains", [P, NG])
        g_mix, g_xq, g_mkv, g_ffn = (gains[:, KT * k:KT * k + KT] for k in range(4))
        pool_scale = gains[:, 4 * KT:NG]
        conv_par = place("conv_par", [P, 4, NF])
        conv_hist = place("conv_hist", [P, 2, NF])
        b_f = place("b_f", [HEADS, 1])
        inv_rms = place("inv_rms", [P, T])
        logf = place("logf", [HEADS, T])
        a_last = place("a_last", [P, 4, NF])
        early_count = place("early_count", [P, 16])
        stat = place("stat", [P, 64])
        phase = here[0]

        v_hi = place("v_hi", [P, NT, DFOX], F32R)
        v_lo = place("v_lo", [P, NT, DFOX], F32R)
        own_hi = place("own_hi", [TS, DFOX], F32R)
        own_lo = place("own_lo", [TS, DFOX], F32R)
        q_hi = place("q_hi", [P, 2, TP], F32R)
        q_lo = place("q_lo", [P, 2, TP], F32R)
        k_hi = place("k_hi", [P, 2, T], F32R)
        k_lo = place("k_lo", [P, 2, T], F32R)
        qs_hi = place("qs_hi", [P, 2, P], F32R)
        qs_lo = place("qs_lo", [P, 2, P], F32R)
        k_new = place("k_new", [P, PAIRS, T])
        decay_p = place("decay_p", [P, 2, 2, TP])
        decay_s = place("decay_s", [P, KEYS])
        prob_p = place("prob_p", [P, 4, TP])
        pt_hi = place("pt_hi", [P, 2, TP], F32R)
        pt_lo = place("pt_lo", [P, 2, TP], F32R)
        vc_hi = place("vc_hi", [P, CT, P], F32R)
        vc_lo = place("vc_lo", [P, CT, P], F32R)
        fox_stat = place("fox_stat", [P, N_ENTRIES, 4])
        prob_s = place("prob_s", [P, KEYS])
        kc_hi = place("kc_hi", [P, PAST], F32R)
        kc_lo = place("kc_lo", [P, PAST], F32R)
        kc_raw = place("kc_raw", [P, CT, P])
        vc_raw = place("vc_raw", [P, CT, P])
        u_all = place("u_all", [P, GROUPS, NHIST + TP + NHIST + TS])
        U_S = NHIST + TP + NHIST
        here[0] = at["decay_p"]
        x_tok = place("x_tok", [P, NT + 1, D])
        xr_tok = place("xr_tok", [P, NT + 1, D])
        square = place("square", [P, D])
        x_gained_s = place("x_gained_s", [P, KT, TS])
        wf_raw = place("wf_raw", [P, KT, HEADS])
        wf_hi = place("wf_hi", [P, KT, P], F32R)
        wf_lo = place("wf_lo", [P, KT, P], F32R)
        cl_tok = place("cl_tok", [P, CT, HEADS])
        rows_in = place("rows_in", [P, 3, P])
        hist_tok = place("hist_tok", [16, DPOOL])
        causal = place("causal", [P, P])
        here[0] = at["prob_p"]
        v_out = place("v_out", [P, NT + 1, DFOX])
        z = place("z", [HEADS, T])
        z_abs = place("z_abs", [HEADS, T])
        z_min = place("z_min", [HEADS, T])
        log_s = place("log_s", [HEADS, KEYS])
        ones_row = place("ones_row", [HEADS, KEYS])
        cum_p = place("cum_p", [HEADS, TP])
        cum_s = place("cum_s", [HEADS, KEYS])
        assert here[0] <= at["wf_raw"]
        here[0] = phase
        x_t = place("x_t", [P, KT, T])
        mem_at = here[0]
        mem_hi = place("mem_hi", [P, KT, MEM], F32R)
        mem_lo = place("mem_lo", [P, KT, MEM], F32R)
        gate_tok = place("gate_tok", [P, NT + 1, HEADS])
        assert here[0] <= at["k_new"]
        here[0] = at["decay_p"]
        sum_a = place("sum_a", [P, U_S + TS])
        sum_b = place("sum_b", [P, U_S + TS])
        diff = place("diff", [P, T])
        diff_hi = place("diff_hi", [P, 2, T], F32R)
        diff_lo = place("diff_lo", [P, 2, T], F32R)
        pool_tok = place("pool_tok", [NHIST, 2, DPOOL])
        assert here[0] <= at["pt_hi"]
        here[0] = at["decay_p"]
        mem_squares = place("mem_squares", [P, MT, D])
        assert here[0] <= at["pool_tok"]
        here[0] = at["pt_hi"]
        wp_raw = place("wp_raw", [P, GROUPS, P])
        wp_hi = place("wp_hi", [P, GROUPS, P], F32R)
        wp_lo = place("wp_lo", [P, GROUPS, P], F32R)
        k_tok = place("k_tok", [P, NT + 1, DFOX])
        assert here[0] <= at["prob_s"]
        here[0] = at["prob_s"]
        x_again = place("x_again", [P, NT + 1, D])
        assert here[0] <= at["u_all"]
        here[0] = slab_bytes - 3 * 4 * T - 96
        gained = place("gained", [P, T])
        squares = place("squares", [P, T])
        square_sum = place("square_sum", [P, T])
        tail = at["gained"]
        here[0] = at["a_hi"]
        mem_tok = place("mem_tok", [P, MT, D])
        here[0] = mem_at
        mp = place("mp", [P, 2, 4, MEM])
        mpt_hi = place("mpt_hi", [P, MT, TP], F32R)
        mpt_lo = place("mpt_lo", [P, MT, TP], F32R)
        here[0] = mem_at + 2 * 4 * KT * MEM
        kv_tok = place("kv_tok", [P, MT, D])
        mk_hi = place("mk_hi", [P, 2, KT, MEM], F32R)
        mk_lo = place("mk_lo", [P, 2, KT, MEM], F32R)
        mv_hi = place("mv_hi", [P, 2, MT, D], F32R)
        mv_lo = place("mv_lo", [P, 2, MT, D], F32R)
        assert here[0] <= tail, (here[0], tail)
        here[0] = mem_at
        GAP = TP + 2
        TE = GAP + 2 + TS
        gate = place("gate", [P, TE])
        up_b = place("up_b", [P, T])
        conv_a = place("conv_a", [P, TE])
        conv_b = place("conv_b", [P, TE])
        silu = place("silu", [P, TE])
        hidden = place("hidden", [P, T])
        par = place("par", [P, 6])
        conv_tok = place("conv_tok", [4 * NF, P])
        y_tok = place("y_tok", [P, NT + 1, D])
        y_junk = place("y_junk", [P, D])
        g_final = place("g_final", [P, D])

        ps = [ctx.enter_context(nc.psum_tensor(f"ps{n}", [P, 2, 512], F32)) for n in range(4)]
        ACC, SC, OB = ps[0:2], ps[2], ps[3]
        TB = [ps[1][:, 0], ps[1][:, 1]]
        MISC = [ps[2][:, 0], ps[2][:, 1], ps[3][:, 0], ps[3][:, 1]]

        def sem(name):
            return ctx.enter_context(nc.semaphore(name))

        weight_landed = [sem("weight_landed0"), sem("weight_landed1")]
        weight_hi_ready, weight_lo_ready, weight_used = sem("weight_hi_ready"), sem("weight_lo_ready"), sem("weight_used")
        acc_free = sem("acc_free")
        x_landed = [sem(f"x_landed{t}") for t in range(NT + 1)]
        rows_landed, small_landed = sem("rows_landed"), sem("small_landed")
        consts_ready, masks_ready, masks_split = sem("consts_ready"), sem("masks_ready"), sem("masks_split")
        x_squared, x_rms, xr_ready = sem("x_squared"), sem("x_rms"), sem("xr_ready")
        cols_turned, cols_ready = sem("cols_turned"), sem("cols_ready")
        hs_turned, hs_gained, h_turned, h_hi_ready, h_lo_ready = (
            sem("hs_turned"), sem("hs_gained"), sem("h_turned"), sem("h_hi_ready"), sem("h_lo_ready"))
        hs_hi_ready = sem("hs_hi_ready")
        v_copied, v_free = sem("v_copied"), sem("v_free")
        window_ready, hs_lo_ready = sem("window_ready"), sem("hs_lo_ready")
        wf_hi_ready, wf_ready = sem("wf_hi_ready"), sem("wf_ready")
        gate_done, gate_act, gate_dve = sem("gate_done"), sem("gate_act"), sem("gate_dve")
        cum_ready, cum_stored = sem("cum_ready"), sem("cum_stored")
        decay_landed = [sem("decay_landed0"), sem("decay_landed1")]
        decay_s_landed = sem("decay_s_landed")
        cache_k_landed, cache_v_landed = sem("cache_k_landed"), sem("cache_v_landed")
        qk_hi_ready = sem("qk_hi_ready")
        scores_done, scores_taken = sem("scores_done"), sem("scores_taken")
        exp_done, prob_ready = sem("exp_done"), sem("prob_ready")
        turn_done, turn_hi_ready, turn_ready = sem("turn_done"), sem("turn_hi_ready"), sem("turn_ready")
        pv_done, o_hi_ready, o_free = sem("pv_done"), sem("o_hi_ready"), sem("o_free")
        vc_hi_ready, vc_ready = sem("vc_hi_ready"), sem("vc_ready")
        misc_landed, mem_landed = sem("misc_landed"), sem("mem_landed")
        wp_landed, wp_hi_ready, wp_ready = sem("wp_landed"), sem("wp_hi_ready"), sem("wp_ready")
        diff_ready, diff_hi_ready, diff_lo_ready = sem("diff_ready"), sem("diff_hi_ready"), sem("diff_lo_ready")
        pool_done, pool_hi_ready = sem("pool_done"), sem("pool_hi_ready")
        misc_turned, misc_taken = sem("misc_turned"), sem("misc_taken")
        mem_gained = sem("mem_gained")
        gained_ready, act_hi_ready, squared = sem("gained_ready"), sem("act_hi_ready"), sem("squared")
        sum_ready, mean_done, root_done, rms_ready = sem("sum_ready"), sem("mean_done"), sem("root_done"), sem("rms_ready")
        mem_stat_act, mem_stat_dve = sem("mem_stat_act"), sem("mem_stat_dve")
        kv_out, kv_free, kv_hi = sem("kv_out"), sem("kv_free"), sem("kv_hi")
        kv_lo = sem("kv_lo")
        kv_stored, ck_landed, cv_landed = sem("kv_stored"), sem("ck_landed"), sem("cv_landed")
        mk_turned, mk_hi_done, mk_ready = sem("mk_turned"), sem("mk_hi_done"), sem("mk_ready")
        mq_hi = sem("mq_hi")
        ms_done, ms_max, ms_exp, ms_prob = sem("ms_done"), sem("ms_max"), sem("ms_exp"), sem("ms_prob")
        mt_done, mt_hi, mt_ready = sem("mt_done"), sem("mt_hi"), sem("mt_ready")
        mo_done, mo_hi, mo_ready = sem("mo_done"), sem("mo_hi"), sem("mo_ready")
        conv_second, mq_ready = sem("conv_second"), sem("mq_ready")
        gate_ready, conv_first, conv_ready, silu_ready = sem("gate_ready"), sem("conv_first"), sem("conv_ready"), sem("silu_ready")
        hidden_ready, hidden_hi = sem("hidden_ready"), sem("hidden_hi")
        hidden_free = sem("hidden_free")
        conv_turned, conv_tok_ready = sem("conv_turned"), sem("conv_tok_ready")
        y_turned, y_squared, y_root, y_ready = sem("y_turned"), sem("y_squared"), sem("y_root"), sem("y_ready")
        g_final_landed = sem("g_final_landed")
        stored, y_stored = sem("stored"), sem("y_stored")
        act_link, dve_link, pool_link = sem("act_link"), sem("dve_link"), sem("pool_link")
        block = ctx.enter_context(nc.Block())

        def halves(acc):
            return acc[:, :, 0:H]

        def by_half(x):
            return x.rearrange("p (h t) -> p h t", h=2)

        def three(mm, out, w, x, first, last):
            mm(out, w[0], x[0], start=first, stop=False)
            mm(out, w[0], x[1], start=False, stop=False)
            return mm(out, w[1], x[0], start=False, stop=last)

        def project(slot, x_hi, x_lo, acc, feature_tiles, total):
            for k in feature_tiles:
                c = slice(k * P, k * P + P)
                for w, x in ((w_hi, x_hi), (w_hi, x_lo), (w_lo, x_hi)):
                    for h in range(2):
                        mm = nc.tensor.matmul(acc[:, h, 0:H], w[slot][:, c], x[:, k, h * H:h * H + H],
                                              start=(k == 0 and w is w_hi and x is x_hi),
                                              stop=(k == total - 1 and w is w_lo))
            if feature_tiles[-1] == total - 1:
                mm.then_inc(weight_used, 1)

        def round_weights(eng, n, slot):
            eng.wait_ge(weight_landed[slot], (n // 2) * 16 + 16 if isinstance(n, int) else n * 8 + (16 - 8 * slot))
            if not isinstance(n, int) or n >= 2:
                eng.wait_ge(weight_used, n - 1)
            nc.scalar.activation(w_hi[slot][:], w_raw[slot][:], ACT.Copy).then_inc(weight_hi_ready, 1)

        def rest_of_weights(eng, n, slot):
            eng.wait_ge(weight_hi_ready, n + 1)
            nc.vector.tensor_tensor(w_lo[slot][:], w_raw[slot][:], w_hi[slot][:].bitcast(F32),
                                    ALU.subtract).then_inc(weight_lo_ready, 1)

        def minus(out, x, hi):
            return nc.vector.tensor_tensor(out, x, hi, ALU.subtract)

        def scaled_minus(out, x, scale, hi):
            return nc.vector.scalar_tensor_tensor(out, x, scale, hi, ALU.mult, ALU.subtract)

        def f32(x):
            return x.bitcast(F32)

        def entry(g):
            j, e = divmod(g, ENTRIES)
            return j, e, e // NT, e % NT

        def keys_of(e):
            return (e % NT + 1) * P if e < 2 * NT else (512 if e < 2 * NT + 2 else TS)

        def probs_done(g):
            j, e = divmod(g, ENTRIES)
            return j * (2 * NT + 1) + min(e, 2 * NT) + 1

        def prompt_slot(g):
            j, e = divmod(g, ENTRIES)
            return (j * 2 * NT + e) % 4

        def prompt_entry_before(g, back):
            j, e = divmod(g, ENTRIES)
            p = j * 2 * NT + e - back
            return None if p < 0 else p // (2 * NT) * ENTRIES + p % (2 * NT)

        def last_prob_turn(t):
            for b in range(t - 2, -1, -2):
                if TURNS[b][0] == "P":
                    return TURNS[b][1]
            return None

        def turns_of(s):
            j, e = divmod(s, ENTRIES)
            found = []
            if j < PAIRS and e in (2, 5):
                found.append(TURN[("K", j, 0 if e == 2 else 1)])
            if s >= LAG and s - LAG < N_ENTRIES:
                found.append(TURN[("P", s - LAG)])
            return found

        OUTPUTS = 3

        def output_of(g):
            j, e = divmod(g, ENTRIES)
            n = e // NT
            return OUTPUTS * j + n, OB[:, n % 2]

        def output_bank_free(n):
            before = {0: n - 1, 1: n - 3, 2: n - 2}[n % OUTPUTS]
            return None if before < 0 else before + 1

        STEPS = N_ENTRIES + LAG + 2
        MISCS = ([("k", t) for t in range(NT + 1)] + [("u", 0), ("u", 1), ("f", 0)]
                 + [("x", k) for k in range(KT)] + [("xs", 0)] + [("m", q) for q in range(4)])
        U_ORDER = [3, 2, 1, 0]
        SAMPLE_MIN = sem("sample_min")

        w_in = a["w_in"][0]
        cols_k = "(k p) c -> p k c"

        def turn_shape(e):
            if e < 2 * NT:
                return P, (e % NT + 1) * P
            return (P, 4 * P) if e < ENTRIES - 1 else (TS, P)

        def output_after(s):
            g = s - LAG - 2
            if g < 0 or g >= N_ENTRIES or g % ENTRIES not in (NT - 1, 2 * NT - 1, ENTRIES - 1):
                return None
            return output_of(g)[0], g

        def output_pieces(n):
            j, m = divmod(n, OUTPUTS)
            bank = OB[:, m % 2]
            k = GROUPS + j
            if m < 2:
                r = slice(m * DH, m * DH + DH)
                return [(lambda x, r=r: x[r, k, 0:TP], bank[r, :])]
            return [(lambda x, h=h: x[h * DH:h * DH + DH, k, TP:T],
                     bank[h * DH:h * DH + DH, h * DH:h * DH + TS]) for h in range(2)]

        def memory_bank(m):
            if m < MH:
                return ACC[m % 2][:]
            return ACC[0][:, 0].rearrange("p (k t) -> p k t", k=KT)

        def memory_output(x, m):
            return x[:, 2 * m:2 * m + 2, 0:TP] if m < MH else x[:, :, TP:T]

        def final_bank(t):
            return ps[(t + 1) % 4]

        @block.sync
        def _(sp):
            for t in range(NT):
                sp.dma_start(x_tok[:, t, :], a["x_prompt"][0, t * P:t * P + P, :]).then_inc(x_landed[t], 16)
            sp.dma_start(x_tok[0:TS, NT, :], a["x_sample"][0]).then_inc(x_landed[NT], 16)

            def load(n, slot, source, shape=None):
                if not isinstance(n, int) or n >= 2:
                    sp.wait_ge(weight_lo_ready, n - 1)
                dst = w_raw[slot][:]
                if shape is not None:
                    dst = dst[:, 0:shape[0] * shape[1]].rearrange("p (k c) -> p k c", k=shape[0])
                sp.dma_start(dst, source).then_inc(weight_landed[slot], 16)

            v_cols = slice(DPOOL + 2 * DFOX, DPOOL + 3 * DFOX)
            for n in range(4):
                load(W_V + n, n % 2, w_in[2 * n * P:2 * n * P + 2 * P, v_cols].rearrange(cols_k, p=P), (2, DFOX))
            for j in range(PAIRS):
                for c in range(2):
                    at_col = DPOOL + c * DFOX + j * P
                    load(W_QK + 2 * j + c, c, w_in[:, at_col:at_col + P].rearrange(cols_k, p=P), (KT, P))
            for n, g in enumerate(U_ORDER):
                load(W_U + n, n % 2, w_in[:, g * P:g * P + P].rearrange(cols_k, p=P), (KT, P))
            sp.wait_ge(turn_done, len(TURNS))
            sp.wait_ge(scores_done, N_ENTRIES)
            sp.wait_ge(vc_ready, PAIRS)
            for t in range(NT):
                sp.dma_start(x_again[:, t, :], a["x_prompt"][0, t * P:t * P + P, :]).then_inc(misc_landed, 16)
            sp.dma_start(x_again[0:TS, NT, :], a["x_sample"][0]).then_inc(misc_landed, 16)

            def by_columns(n0, w, k=KT, off=(0, P), step=2 * P, rounds=KT // 2):
                source = w.rearrange(cols_k, p=P)
                with sp.Fori(0, rounds) as i:
                    for c in range(2):
                        load(i * 2 + (n0 + c), c, source[:, :, bass.ds(i * step + off[c], P)], (k, P))

            def by_rows(n0, w, r0, rounds):
                with sp.Fori(0, rounds) as i:
                    for c in range(2):
                        load(i * 2 + (n0 + c), c, w[bass.ds(i * (2 * P) + (r0 + c) * P, P), :])

            by_columns(W_O, a["w_o"][0])
            by_rows(W_MK, a["w_mk"][0], 0, KT // 2)
            by_columns(W_MQ, a["w_mq"][0])
            by_rows(W_MV, a["w_mv"][0], 0, KT // 2)
            by_columns(W_MO, a["w_mo"][0])
            for k, (f0, nf) in enumerate(CHUNKS):
                by_columns(W_UP[k], a["w_up"][0], off=(f0 * P, DFF + f0 * P), step=P, rounds=nf)
                by_columns(W_DOWN[k], a["w_down"][0, f0 * P:(f0 + nf) * P, :], k=nf)
            for t in range(NT + 1):
                sp.wait_ge(y_ready, t + 1)
                y = o["y_prompt"][0, t * P:t * P + P, :] if t < NT else o["y_sample"][0]
                sp.dma_start(y, y_tok[0:y.shape[0], t, :]).then_inc(y_stored, 16)
            sp.wait_ge(y_stored, 16 * (NT + 1))
            N_STORED = 2 + 2 + 2 + 2 + 2 + 2
            sp.wait_ge(stored, 16 * N_STORED)

        @block.gpsimd
        def _(pool):
            link = Tally(pool_link)

            def after(ins):
                link.inc(ins)
                pool.wait_ge(pool_link, link.now)

            def small(dst, src):
                pool.dma_start(dst, src).then_inc(small_landed, 16)

            n = 0
            for name in ("g_mix", "g_xq", "g_mkv", "g_ffn"):
                pool.dma_start(rows_in[n:n + KT, 0, :], a[name][0].rearrange("(k p) -> k p", p=P)).then_inc(rows_landed, 16)
                n += KT
            pool.dma_start(rows_in[n:NG, 0, :], a["pool_scale"][0].rearrange("(k p) -> k p", p=P)).then_inc(rows_landed, 16)
            pool.dma_start(rows_in[0:3 * NF, 1, :], a["conv_w"][0].rearrange("j (f p) -> (j f) p", p=P)).then_inc(rows_landed, 16)
            pool.dma_start(rows_in[3 * NF:4 * NF, 1, :], a["conv_b"][0].rearrange("(f p) -> f p", p=P)).then_inc(rows_landed, 16)
            pool.dma_start(rows_in[0:2 * NF, 2, :], a["state_ffn_conv"][0, 0].rearrange("s (f p) -> (s f) p", p=P)).then_inc(rows_landed, 16)
            pool.dma_start(hist_tok[0:NHIST, :], a["state_pool"][0, 0]).then_inc(rows_landed, 16)
            after(nc.gpsimd.memset(ident[:], 0.0))
            nc.gpsimd.affine_select(out=ident[:], in_=ident[:], compare_op=ALU.not_equal, fill=1.0, base=0,
                                    pattern=[[-1, P]], channel_multiplier=1).then_inc(consts_ready, 1)
            nc.gpsimd.memset(eps[:], EPS).then_inc(consts_ready, 1)
            nc.gpsimd.memset(one[:], 1.0).then_inc(consts_ready, 1)
            nc.gpsimd.memset(mean_w[:], 1.0 / D).then_inc(consts_ready, 1)
            nc.gpsimd.memset(stat[:], 1.0).then_inc(consts_ready, 1)
            for x in flat_a + flat_b:
                nc.gpsimd.memset(f32(x[:, KT * T:]), 0.0).then_inc(consts_ready, 1)
            for x in (wf_hi, wf_lo, qs_hi, qs_lo):
                nc.gpsimd.memset(f32(x[:]), 0.0).then_inc(consts_ready, 1)
            small(wf_raw[:], w_in[:, D_IN - HEADS:D_IN].rearrange(cols_k, p=P))
            small(b_f[:], a["b_f"][0].rearrange("(h x) -> h x", x=1))
            small(cl_tok[:], a["cache_fox_logf"][0, 0].rearrange("(c p) h -> p c h", p=P))
            after(nc.gpsimd.memset(causal[:], 0.0))
            nc.gpsimd.affine_select(out=causal[:], in_=causal[:], compare_op=ALU.is_ge, fill=MASKED, base=0,
                                    pattern=[[-1, P]], channel_multiplier=1).then_inc(masks_ready, 1)
            for t in range(16):
                nc.gpsimd.memset(early_count[:, t:t + 1], 1.0 / (t + 1))
            pool.wait_ge(cols_turned, 1)
            nc.gpsimd.memset(u_all[:, :, 0:NHIST], 0.0).then_inc(masks_ready, 1)
            pool.wait_ge(v_copied, NT + 1)
            pool.dma_start(o["fox_v_prompt"][0, 0].rearrange("(t p) h d -> p t (h d)", p=P), v_out[:, 0:NT, :]).then_inc(stored, 16)
            pool.dma_start(o["fox_v_sample"][0, 0].rearrange("t h d -> t (h d)"), v_out[0:TS, NT, :]).then_inc(stored, 16)
            pool.wait_ge(cum_ready, 2)
            pool.dma_start(decay_p_dram, cum_p[:]).then_inc(cum_stored, 16)
            pool.dma_start(decay_s_dram, cum_s[:]).then_inc(cum_stored, 16)
            pool.wait_ge(cum_stored, 32)
            pool.wait_ge(stored, 32)

            def load_decay_prompt(j):
                if j >= 2:
                    pool.wait_ge(scores_taken, ENTRIES * (j - 2) + 2 * NT)
                for h in range(2):
                    row = decay_p_dram[2 * j + h:2 * j + h + 1, :]
                    pool.dma_start(decay_p[:, j % 2, h, :], row.partition_broadcast(P)).then_inc(decay_landed[j % 2], 16)

            def load_sample(j):
                if j >= 1:
                    pool.wait_ge(scores_taken, ENTRIES * j)
                for h in range(2):
                    row = decay_s_dram[2 * j + h:2 * j + h + 1, :]
                    pool.dma_start(decay_s[h * DH:h * DH + DH, :], row.partition_broadcast(DH)).then_inc(decay_s_landed, 16)

            def load_cache(j):
                heads = slice(2 * j, 2 * j + 2)
                if j >= 1:
                    pool.wait_ge(turn_done, TURN[("K", j - 1, 1)] + 1)
                pool.dma_start(kc_raw[:], a["cache_fox_k"][0, 0, :, heads, :].rearrange("(c p) h d -> p c (h d)", p=P)).then_inc(cache_k_landed, 16)
                if j >= 1:
                    pool.wait_ge(vc_ready, j)
                pool.dma_start(vc_raw[:], a["cache_fox_v"][0, 0, :, heads, :].rearrange("(c p) h d -> p c (h d)", p=P)).then_inc(cache_v_landed, 16)

            load_decay_prompt(0)
            load_cache(0)
            load_sample(0)
            load_decay_prompt(1)
            for j in range(1, PAIRS):
                load_cache(j)
                load_sample(j)
                if j + 1 < PAIRS:
                    load_decay_prompt(j + 1)
            pool.wait_ge(scores_taken, N_ENTRIES)
            pool.wait_ge(pv_done, N_ENTRIES)
            pool.dma_start(wp_raw[:], a["w_pool"][0].rearrange("g c d -> c g d")).then_inc(wp_landed, 16)
            L = U_S + TS
            for n, g in enumerate(U_ORDER):
                pool.wait_ge(acc_free, A_U + n + 1)
                src = u_all[:, g, :]
                for k in range(g + 1):
                    dst = (sum_a, sum_b)[k % 2]
                    lo = 2 ** (k + 1) - 1
                    if k == 0 and n >= 1:
                        pool.wait_ge(diff_ready, n)
                    ins = nc.gpsimd.tensor_tensor(dst[:, lo:L], src[:, lo:L], src[:, lo - 2 ** k:L - 2 ** k], ALU.add)
                    if k < g:
                        after(ins)
                    else:
                        ins.then_inc(window_ready, 1)
                    src = dst[:]
            pool.wait_ge(weight_used, W_O)
            pool.dma_start(mem_tok[:], a["mem_prompt"][0].rearrange("(t p) d -> p t d", p=P)).then_inc(mem_landed, 16)
            pool.wait_ge(misc_taken, NT + 1)
            pool.dma_start(o["fox_k_prompt"][0, 0].rearrange("(t p) h d -> p t (h d)", p=P), k_tok[:, 0:NT, :]).then_inc(stored, 16)
            pool.dma_start(o["fox_k_sample"][0, 0].rearrange("t h d -> t (h d)"), k_tok[0:TS, NT, :]).then_inc(stored, 16)
            pool.wait_ge(misc_taken, NT + 4)
            pool.dma_start(o["pool_state_prompt"][0, 0], pool_tok[:, 0, :]).then_inc(stored, 16)
            pool.dma_start(o["pool_state_sample"][0, 0], pool_tok[:, 1, :]).then_inc(stored, 16)
            pool.dma_start(o["fox_logf_prompt"][0, 0].rearrange("(t p) h -> p t h", p=P), gate_tok[:, 0:NT, :]).then_inc(stored, 16)
            pool.dma_start(o["fox_logf_sample"][0, 0], gate_tok[0:TS, NT, :]).then_inc(stored, 16)
            pool.wait_ge(kv_out, 2)
            pool.dma_start(o["mem_k_prompt"][0, 0].rearrange("(t p) h d -> p t (h d)", p=P), kv_tok[:]).then_inc(stored, 16)
            pool.wait_ge(stored, 16 * 9)
            pool.wait_ge(mk_turned, 4)
            pool.dma_start(kv_tok[:], a["cache_mem_k"][0, 0].rearrange("(t p) h d -> p t (h d)", p=P)).then_inc(ck_landed, 16)
            pool.wait_ge(kv_out, 4)
            pool.dma_start(o["mem_v_prompt"][0, 0].rearrange("(t p) h d -> p t (h d)", p=P), kv_tok[:]).then_inc(stored, 16)
            pool.wait_ge(stored, 16 * 10)
            pool.wait_ge(kv_lo, 1)
            pool.dma_start(kv_tok[:], a["cache_mem_v"][0, 0].rearrange("(t p) h d -> p t (h d)", p=P)).then_inc(cv_landed, 16)
            for k, (f0, nf) in enumerate(CHUNKS):
                with pool.Fori(0, nf) as i:
                    pool.wait_ge(silu_ready, i + (f0 + 1))
                    pool.wait_ge(acc_free, i * 2 + (A_UP[k] + 2))
                    pool.wait_ge(hidden_free, i + (f0 + 1))
                    nc.gpsimd.tensor_tensor(hidden[:, 0:TP], silu[:, 0:TP], up_b[:, 0:TP], ALU.mult)
                    nc.gpsimd.tensor_tensor(hidden[:, TP:T], silu[:, GAP:GAP + TS], up_b[:, TP:T], ALU.mult).then_inc(hidden_ready, 1)
            pool.dma_start(g_final[:], a["g_final"].rearrange("(x d) -> x d", x=1).partition_broadcast(P)).then_inc(g_final_landed, 16)
            pool.wait_ge(conv_tok_ready, 1)
            pool.dma_start(o["conv_state_prompt"][0, 0].rearrange("s (f p) -> (s f) p", p=P), conv_tok[0:2 * NF, :]).then_inc(stored, 16)
            pool.dma_start(o["conv_state_sample"][0, 0].rearrange("s (f p) -> (s f) p", p=P), conv_tok[2 * NF:4 * NF, :]).then_inc(stored, 16)

        @block.scalar
        def _(act):
            link = Tally(act_link)

            def after(ins):
                link.inc(ins)
                act.wait_ge(act_link, link.now)

            def copy(out, x, scale=1.0):
                return nc.scalar.activation(out, x, ACT.Copy, scale=scale)

            act.wait_ge(consts_ready, 13)
            for t in range(NT + 1):
                r = P if t < NT else TS
                act.wait_ge(x_landed[t], 16)
                if t >= 1:
                    act.wait_ge(x_squared, t)
                nc.scalar.activation(square[0:r, :], x_tok[0:r, t, :], ACT.Square,
                                     accum_out=stat[0:r, t:t + 1]).then_inc(x_squared, 1)
            act.wait_ge(x_squared, NT + 1)
            nc.scalar.activation(stat[:, 8:8 + NT + 1], stat[:, 0:NT + 1], ACT.Sqrt, bias=eps[:],
                                 scale=1.0 / D).then_inc(x_rms, 1)
            act.wait_ge(small_landed, 48)
            copy(wf_hi[:, :, 0:HEADS], wf_raw[:]).then_inc(wf_hi_ready, 1)
            round_weights(act, 0, 0)
            round_weights(act, 1, 1)
            act.wait_ge(cols_ready, 4)
            act.wait_ge(hs_gained, 1)
            copy(a_hi[:, :, TP:T], x_gained_s[:]).then_inc(hs_hi_ready, 1)
            for k in range(KT):
                act.wait_ge(h_turned, k + 1)
                copy(a_hi[:, k, 0:TP], (SC[:, 1], OB[:, 0])[k % 2], g_mix[:, k:k + 1]).then_inc(h_hi_ready, 1)
                if k in (3, 5):
                    round_weights(act, (k + 1) // 2, (k + 1) // 2 % 2)
            round_weights(act, 4, 0)
            round_weights(act, 5, 1)
            act.wait_ge(weight_used, 4)
            for t in (NT, 0, 1, 2, 3):
                r = P if t < NT else TS
                bank = (ACC[t // 2][:, t % 2] if t < NT else SC[0:TS, 0])
                copy(v_hi[:, t, :] if t < NT else own_hi[:], bank)
                copy(v_out[0:r, t, :], bank).then_inc(v_copied, 1)
            act.wait_ge(gate_dve, 1)
            after(nc.scalar.activation(z_abs[:], z[:], ACT.Abs))
            after(nc.scalar.activation(z_abs[:], z_abs[:], ACT.Exp, scale=-1.0))
            nc.scalar.activation(z_abs[:], z_abs[:], ACT.Ln, bias=one[0:HEADS]).then_inc(gate_act, 1)

            def finish_q(j):
                n, b, acc = W_QK + 2 * j, j % 2, ACC[0]
                act.wait_ge(weight_used, n + 1)
                if j >= 2:
                    act.wait_ge(scores_done, ENTRIES * (j - 1))
                copy(q_hi[:, b, 0:H], acc[:, 0, 0:H], QSCALE)
                copy(q_hi[:, b, H:TP], acc[:, 1, 0:TP - H], QSCALE)
                for h in range(2):
                    r = slice(h * DH, h * DH + DH)
                    ins = copy(qs_hi[r, b, h * DH:h * DH + DH], acc[r, 1, TP - H:H], QSCALE)
                ins.then_inc(qk_hi_ready, 1)

            def finish_k(j):
                n, b, acc = W_QK + 2 * j + 1, j % 2, ACC[0]
                act.wait_ge(weight_used, n + 1)
                copy(by_half(k_hi[:, b, :]), halves(acc))
                copy(by_half(k_new[:, j, :]), halves(acc)).then_inc(qk_hi_ready, 1)

            round_weights(act, 6, 0)
            finish_q(0)
            round_weights(act, 7, 1)
            finish_k(0)

            for s in range(STEPS):
                j, e = divmod(s, ENTRIES)
                if e in (5, 10) and j < PAIRS:
                    n = W_QK + 2 * (j + 1) + e // 10
                    round_weights(act, n + 2, n % 2)
                    if j + 1 < PAIRS:
                        (finish_q, finish_k)[e // 10](j + 1)
                if e == 6 and j < PAIRS:
                    act.wait_ge(cache_v_landed, 16 * (j + 1))
                    if j >= 1:
                        act.wait_ge(pv_done, ENTRIES * j)
                    copy(vc_hi[:], vc_raw[:]).then_inc(vc_hi_ready, 1)
                if s < N_ENTRIES:
                    if e < 2 * NT:
                        act.wait_ge(scores_taken, s + 1)
                        p = prob_p[:, prompt_slot(s), 0:keys_of(e)]
                        nc.scalar.activation(p, p, ACT.Exp, bias=fox_stat[:, s, 0:1], scale=-1.0,
                                             accum_out=fox_stat[:, s, 1:2]).then_inc(exp_done, 1)
                    elif e == ENTRIES - 1:
                        act.wait_ge(SAMPLE_MIN, j + 1)
                        nc.scalar.activation(prob_s[:], prob_s[:], ACT.Exp, bias=fox_stat[:, s, 3:4],
                                             scale=-1.0, accum_out=fox_stat[:, s, 1:2]).then_inc(exp_done, 1)
                for t in turns_of(s):
                    what = TURNS[t]
                    act.wait_ge(turn_done, t + 1)
                    if what[0] == "K":
                        if what[1] >= 1:
                            act.wait_ge(scores_done, ENTRIES * what[1])
                        copy(kc_hi[:, what[2] * 512:what[2] * 512 + 512], TB[t % 2]).then_inc(turn_hi_ready, 1)
                    else:
                        e_t = what[1] % ENTRIES
                        rows, width = turn_shape(e_t)
                        if last_prob_turn(t) is not None:
                            act.wait_ge(pv_done, last_prob_turn(t) + 1)
                        copy(pt_hi[0:rows, t % 2, 0:width], TB[t % 2][0:rows, 0:width]).then_inc(turn_hi_ready, 1)
                out = output_after(s)
                if out is not None:
                    n, g = out
                    act.wait_ge(pv_done, g + 1)
                    for d, b in output_pieces(n):
                        ins = copy(d(b_hi), b)
                    ins.then_inc(o_hi_ready, 1)
            round_weights(act, W_U + 4, 0)
            act.wait_ge(wp_landed, 16)
            copy(wp_hi[:], wp_raw[:]).then_inc(wp_hi_ready, 1)
            round_weights(act, W_U + 5, 1)
            for n, g in enumerate(U_ORDER):
                act.wait_ge(diff_ready, n + 1)
                if n >= 2:
                    act.wait_ge(pool_done, n - 1)
                copy(diff_hi[:, n % 2, :], diff[:]).then_inc(diff_hi_ready, 1)
            for n, g in enumerate(U_ORDER):
                act.wait_ge(pool_done, n + 1)
                copy(by_half(b_hi[:, g, :]), halves(ACC[n % 2]), pool_scale[:, g:g + 1]).then_inc(pool_hi_ready, 1)
            for n, (kind, m) in enumerate(MISCS):
                bank = MISC[n % 4]
                act.wait_ge(misc_turned, n + 1)
                if kind == "k":
                    r = P if m < NT else TS
                    ins = copy(k_tok[0:r, m, :], bank[0:r, :])
                elif kind == "u":
                    ins = copy(pool_tok[:, m, :], bank[0:NHIST, :])
                elif kind == "f":
                    ins = copy(gate_tok[:], bank[:, 0:(NT + 1) * HEADS].rearrange("p (t h) -> p t h", h=HEADS))
                elif kind == "x":
                    ins = copy(x_t[:, m, 0:TP], bank)
                elif kind == "xs":
                    ins = copy(x_t[:, :, TP:T], bank.rearrange("p (k t) -> p k t", k=KT))
                else:
                    for c in range(2):
                        k = 2 * m + c
                        ins = copy(mem_hi[:, k, :], bank[:, c * MEM:c * MEM + MEM], g_mkv[:, k:k + 1])
                ins.then_inc(misc_taken, 1)

            for t in range(MT):
                ins = nc.scalar.activation(mem_squares[:, t, :], mem_tok[:, t, :], ACT.Square,
                                           accum_out=stat[:, 16 + t:17 + t])
                link.inc(ins)
            act.wait_ge(act_link, link.now)
            nc.scalar.activation(stat[:, 18:20], stat[:, 16:18], ACT.Sqrt, bias=eps[:],
                                 scale=1.0 / D).then_inc(mem_stat_act, 1)

            def residual_steps(w0, first, sums):
                with act.Fori(0, KT // 2) as i:
                    for c in range(2):
                        k = i * 2 + c
                        round_weights(act, k + (w0 + 2), c)
                        act.wait_ge(gained_ready, k + (first + 1))
                        copy((a_hi if first == 0 else b_hi)[:, bass.ds(k, 1), :].rearrange("p k t -> p (k t)"),
                             gained[:]).then_inc(act_hi_ready, 1)
                        act.wait_ge(sum_ready, k + sums)
                        nc.scalar.activation(squares[:], x_t[:, bass.ds(k, 1), :].rearrange("p k t -> p (k t)"),
                                             ACT.Square).then_inc(squared, 1)

            def root(n, bank):
                act.wait_ge(mean_done, n)
                nc.scalar.activation(by_half(inv_rms[:]), bank[:, :, 0:H], ACT.Sqrt, bias=eps[:]).then_inc(root_done, 1)

            residual_steps(W_O, 0, 1)
            with act.Fori(0, 2) as i:
                for c in range(2):
                    round_weights(act, i * 2 + (W_MK + 2 + c), c)
            root(1, ACC[0])
            with act.Fori(0, 2) as i:
                for c in range(2):
                    round_weights(act, i * 2 + (W_MK + 6 + c), c)
            act.wait_ge(mem_stat_dve, 1)
            act.wait_ge(stored, 16 * 8)
            for t in range(MT):
                copy(kv_tok[:, t, :].rearrange("p (b c) -> p b c", b=2), (SC, OB)[t][:], stat[:, 20 + t:21 + t]).then_inc(kv_out, 1)
            with act.Fori(0, KT // 2) as i:
                for c in range(2):
                    k = i * 2 + c
                    round_weights(act, k + (W_MQ + 2), c)
                    act.wait_ge(acc_free, k + (A_MQ + 1))
                    copy(b_hi[:, bass.ds(k, 1), :].rearrange("p k t -> p (k t)"), gained[:], MSCALE).then_inc(mq_hi, 1)

            def memory_keys(s):
                for q in range(4):
                    act.wait_ge(mk_turned, 4 * s + q + 1)
                    copy(mk_hi[:, s, 2 * q:2 * q + 2, :], ACC[q // 2][:, q % 2].rearrange("p (k m) -> p k m", k=2)).then_inc(mk_hi_done, 1)

            memory_keys(0)
            with act.Fori(0, 2) as i:
                for c in range(2):
                    round_weights(act, i * 2 + (W_MV + 2 + c), c)
            memory_keys(1)
            with act.Fori(0, 2) as i:
                for c in range(2):
                    round_weights(act, i * 2 + (W_MV + 6 + c), c)
            act.wait_ge(weight_used, W_MV + KT)
            for t in range(MT):
                bank = (SC, OB)[t]
                copy(kv_tok[:, t, :].rearrange("p (b c) -> p b c", b=2), bank[:], stat[:, 20 + t:21 + t]).then_inc(kv_out, 1)
            act.wait_ge(kv_out, 4)
            copy(mv_hi[:, 0], kv_tok[:]).then_inc(kv_hi, 1)
            act.wait_ge(cv_landed, 16)
            copy(mv_hi[:, 1], kv_tok[:]).then_inc(kv_hi, 1)

            for s in range(MH + 1 + 2):
                if s <= MH:
                    r = P if s < MH else TS
                    act.wait_ge(ms_max, s + 1)
                    for q in range(4):
                        ins = nc.scalar.activation(mp[0:r, s % 2, q, :], SC[0:r, q // 2, q % 2 * MEM:q % 2 * MEM + MEM], ACT.Exp,
                                                   bias=stat[0:r, 28 + q:29 + q], accum_out=stat[0:r, 32 + q:33 + q])
                    ins.then_inc(ms_exp, 1)
                if s >= 2:
                    m = s - 2
                    act.wait_ge(mo_done, m + 1)
                    copy(memory_output(a_hi, m), memory_bank(m)).then_inc(mo_hi, 1)
                if 1 <= s <= MH + 1:
                    m = s - 1
                    w = TP if m < MH else MH * TS
                    act.wait_ge(mt_done, m + 1)
                    copy(mpt_hi[:, :, 0:w], OB[:, :, 0:w]).then_inc(mt_hi, 1)

            residual_steps(W_MO, KT, KT + 2)
            root(2, SC)
            for k, (f0, nf) in enumerate(CHUNKS):
                with act.Fori(0, nf) as i:
                    round_weights(act, i * 2 + (W_UP[k] + 2), 0)
                    act.wait_ge(gate_ready, i + (f0 + 1))
                    nc.scalar.activation(conv_a[:, 2:TE], gate[:, 2:TE], ACT.Identity, bias=par[:, 3:4],
                                         scale=par[:, 2:3]).then_inc(conv_first, 1)
                    act.wait_ge(conv_ready, i + (f0 + 1))
                    act.wait_ge(hidden_free, i + (f0 + 1))
                    nc.scalar.activation(silu[:, 0:TE - 2], conv_a[:, 2:TE], ACT.Silu).then_inc(silu_ready, 1)
                    round_weights(act, i * 2 + (W_UP[k] + 3), 1)
                    act.wait_ge(hidden_ready, i + (f0 + 1))
                    copy(a_hi[:, bass.ds(i, 1), :].rearrange("p k t -> p (k t)"), hidden[:]).then_inc(hidden_hi, 1)
                with act.Fori(0, KT // 2 - (k == 2)) as i:
                    for c in range(2):
                        round_weights(act, i * 2 + (W_DOWN[k] + 2 + c), c)
            act.wait_ge(conv_turned, 1)
            copy(conv_tok[:], MISC[0][0:4 * NF, 0:P]).then_inc(conv_tok_ready, 1)
            for t in range(NT + 1):
                r = P if t < NT else TS
                act.wait_ge(y_turned, t + 1)
                nc.scalar.activation(y_junk[0:r, :].rearrange("p (b c) -> p b c", b=2), final_bank(t)[0:r], ACT.Square,
                                     accum_out=stat[0:r, 40 + t:41 + t]).then_inc(y_squared, 1)
                act.wait_ge(y_squared, t + 1)
                nc.scalar.activation(stat[0:r, 48 + t:49 + t], stat[0:r, 40 + t:41 + t], ACT.Sqrt, bias=eps[0:r],
                                     scale=1.0 / D).then_inc(y_root, 1)

        @block.vector
        def _(dve):
            link = Tally(dve_link)
            add, mult, sub = ALU.add, ALU.mult, ALU.subtract

            def after(ins):
                link.inc(ins)
                dve.wait_ge(dve_link, link.now)

            dve.wait_ge(consts_ready, 13)
            nc.vector.tensor_copy(ident_r[:], ident[:]).then_inc(masks_split, 1)
            dve.wait_ge(masks_ready, 1)
            nc.vector.tensor_copy(causal_r[:], causal[:]).then_inc(masks_split, 1)
            for h in range(2):
                r = slice(h * DH, h * DH + DH)
                nc.vector.tensor_copy(causal_s[r, :], causal[r, r]).then_inc(masks_split, 1)
            dve.wait_ge(cols_turned, 1)
            bank = OB[:, 1]
            nc.vector.tensor_copy(gains[:], bank[:, 0:NG]).then_inc(cols_ready, 1)
            nc.vector.tensor_copy(conv_par[:].rearrange("p j f -> p (j f)"), bank[:, 64:64 + 4 * NF]).then_inc(cols_ready, 1)
            nc.vector.tensor_copy(conv_hist[:].rearrange("p s f -> p (s f)"), bank[:, 192:192 + 2 * NF]).then_inc(cols_ready, 1)
            dve.wait_ge(masks_ready, 2)
            nc.vector.tensor_copy(u_all[:, :, NHIST + TP:U_S],
                                  bank[:, 256:256 + 16 * GROUPS].rearrange("p (g t) -> p g t", t=16)[:, :, 0:NHIST]).then_inc(cols_ready, 1)
            dve.wait_ge(x_rms, 1)
            after(nc.vector.reciprocal(stat[:, 56:57 + NT], stat[:, 8:9 + NT]))
            for t in range(NT + 1):
                r = P if t < NT else TS
                nc.vector.tensor_scalar(xr_tok[0:r, t, :], x_tok[0:r, t, :], stat[0:r, 56 + t:57 + t], None,
                                        mult).then_inc(xr_ready, 1)
            dve.wait_ge(wf_hi_ready, 1)
            minus(wf_lo[:, :, 0:HEADS], wf_raw[:], f32(wf_hi[:, :, 0:HEADS])).then_inc(wf_ready, 1)
            dve.wait_ge(hs_turned, 1)
            nc.vector.tensor_tensor(x_gained_s[:], OB[:, 1].rearrange("p (k t) -> p k t", k=KT),
                                    g_mix.unsqueeze(2).to_broadcast([P, KT, TS]), mult).then_inc(hs_gained, 1)
            rest_of_weights(dve, 0, 0)
            rest_of_weights(dve, 1, 1)
            dve.wait_ge(hs_hi_ready, 1)
            minus(a_lo[:, :, TP:T], x_gained_s[:], f32(a_hi[:, :, TP:T])).then_inc(hs_lo_ready, 1)
            for k in range(KT):
                dve.wait_ge(h_hi_ready, k + 1)
                scaled_minus(a_lo[:, k, 0:TP], (SC[:, 1], OB[:, 0])[k % 2], g_mix[:, k:k + 1],
                             f32(a_hi[:, k, 0:TP])).then_inc(h_lo_ready, 1)
                if k in (3, 5):
                    rest_of_weights(dve, (k + 1) // 2, (k + 1) // 2 % 2)
            rest_of_weights(dve, 4, 0)
            rest_of_weights(dve, 5, 1)
            for n, t in enumerate((NT, 0, 1, 2, 3)):
                bank = (ACC[t // 2][:, t % 2] if t < NT else SC[0:TS, 0])
                lo, hi = (v_lo[:, t, :], v_hi[:, t, :]) if t < NT else (own_lo[:], own_hi[:])
                dve.wait_ge(v_copied, n + 1)
                minus(lo, bank, f32(hi)).then_inc(v_free, 1)
            dve.wait_ge(gate_done, 1)
            nc.vector.tensor_scalar(by_half(z[:]), OB[0:HEADS, :, 0:H], b_f[:], None, add).then_inc(gate_dve, 1)
            dve.wait_ge(gate_dve, 1)
            after(nc.vector.tensor_scalar(z_min[:], z[:], 0.0, None, ALU.min))
            after(nc.vector.memset(ones_row[:], 1.0))
            dve.wait_ge(gate_act, 1)
            after(minus(logf[:], z_min[:], z_abs[:]))
            dve.wait_ge(gate_done, 2)
            nc.vector.tensor_copy(log_s[:, 0:PAST].rearrange("h (b t) -> h b t", b=2), SC[0:HEADS]).then_inc(gate_dve, 1)
            nc.vector.tensor_copy(log_s[:, PAST:KEYS], logf[:, TP:T]).then_inc(gate_dve, 1)
            dve.wait_ge(gate_dve, 3)
            nc.vector.tensor_tensor_scan(cum_p[:], ones_row[:, 0:TP], logf[:, 0:TP], 0.0, mult, sub).then_inc(cum_ready, 1)
            nc.vector.tensor_tensor_scan(cum_s[:], ones_row[:], log_s[:], 0.0, mult, sub).then_inc(cum_ready, 1)

            def finish_q(j):
                b, acc = j % 2, ACC[0]
                dve.wait_ge(qk_hi_ready, 2 * j + 1)
                scaled_minus(q_lo[:, b, 0:H], acc[:, 0, 0:H], QSCALE, f32(q_hi[:, b, 0:H]))
                scaled_minus(q_lo[:, b, H:TP], acc[:, 1, 0:TP - H], QSCALE, f32(q_hi[:, b, H:TP]))
                for h in range(2):
                    r = slice(h * DH, h * DH + DH)
                    ins = scaled_minus(qs_lo[r, b, r], acc[r, 1, TP - H:H], QSCALE, f32(qs_hi[r, b, r]))
                ins.then_inc(acc_free, 1)

            def finish_k(j):
                b, acc = j % 2, ACC[0]
                dve.wait_ge(qk_hi_ready, 2 * j + 2)
                minus(by_half(k_lo[:, b, :]), halves(acc), by_half(f32(k_hi[:, b, :]))).then_inc(acc_free, 1)

            def finish_u(n, slot):
                g, acc = U_ORDER[n], ACC[slot]
                dve.wait_ge(weight_used, W_U + n + 1)
                nc.vector.tensor_copy(u_all[:, g, NHIST:NHIST + H], acc[:, 0, 0:H])
                nc.vector.tensor_copy(u_all[:, g, NHIST + H:NHIST + TP], acc[:, 1, 0:TP - H])
                nc.vector.tensor_copy(u_all[:, g, U_S:U_S + TS], acc[:, 1, TP - H:H]).then_inc(acc_free, 1)

            rest_of_weights(dve, 6, 0)
            finish_q(0)
            rest_of_weights(dve, 7, 1)
            finish_k(0)

            for s in range(STEPS):
                j, e = divmod(s, ENTRIES)
                if e in (5, 10) and j < PAIRS:
                    n = W_QK + 2 * (j + 1) + e // 10
                    rest_of_weights(dve, n + 2, n % 2)
                    if j + 1 < PAIRS:
                        (finish_q, finish_k)[e // 10](j + 1)
                    else:
                        finish_u(e // 10, 0)
                if s < N_ENTRIES:
                    dve.wait_ge(scores_done, s + 1)
                    if e == 0:
                        dve.wait_ge(decay_landed[j % 2], 32 * (j // 2 + 1))
                    if e < 2 * NT:
                        before = prompt_entry_before(s, 4)
                        if before is not None:
                            dve.wait_ge(turn_done, TURN[("P", before)] + 1)
                        w = keys_of(e)
                        nc.vector.tensor_tensor_reduce(
                            prob_p[:, prompt_slot(s), 0:w], SC[:, s % 2, 0:w], decay_p[:, j % 2, e // NT, 0:w],
                            -1.0, 3e38, add, ALU.min, fox_stat[:, s, 0:1]).then_inc(scores_taken, 1)
                    else:
                        c = e - 2 * NT
                        if c == 0:
                            dve.wait_ge(decay_s_landed, 32 * (j + 1))
                            if j >= 1:
                                dve.wait_ge(turn_done, TURN[("P", ENTRIES * j - 1)] + 1)
                        w = keys_of(e)
                        nc.vector.tensor_tensor_reduce(
                            prob_s[:, c * 512:c * 512 + w], SC[:, s % 2, 0:w], decay_s[:, c * 512:c * 512 + w],
                            -1.0, 3e38, add, ALU.min, fox_stat[:, s, 0:1]).then_inc(scores_taken, 1)
                        if c == 2:
                            dve.wait_ge(scores_taken, s + 1)
                            nc.vector.tensor_reduce(fox_stat[:, s, 3:4], fox_stat[:, s - 2:s + 1, 0], X,
                                                    ALU.min).then_inc(SAMPLE_MIN, 1)
                if e == 7 and j < PAIRS:
                    dve.wait_ge(vc_hi_ready, j + 1)
                    minus(vc_lo[:], vc_raw[:], f32(vc_hi[:])).then_inc(vc_ready, 1)
                g = s - 1
                if 0 <= g < N_ENTRIES and (g % ENTRIES < 2 * NT or g % ENTRIES == ENTRIES - 1):
                    dve.wait_ge(exp_done, probs_done(g))
                    after(nc.vector.reciprocal(fox_stat[:, g, 2:3], fox_stat[:, g, 1:2]))
                    p = (prob_p[:, prompt_slot(g), 0:keys_of(g % ENTRIES)] if g % ENTRIES < 2 * NT else prob_s[:])
                    nc.vector.tensor_scalar(p, p, fox_stat[:, g, 2:3], None, mult).then_inc(prob_ready, 1)
                for t in turns_of(s):
                    what = TURNS[t]
                    dve.wait_ge(turn_hi_ready, t + 1)
                    if what[0] == "K":
                        c = slice(what[2] * 512, what[2] * 512 + 512)
                        minus(kc_lo[:, c], TB[t % 2], f32(kc_hi[:, c])).then_inc(turn_ready, 1)
                    else:
                        rows, w = turn_shape(what[1] % ENTRIES)
                        minus(pt_lo[0:rows, t % 2, 0:w], TB[t % 2][0:rows, 0:w],
                              f32(pt_hi[0:rows, t % 2, 0:w])).then_inc(turn_ready, 1)
                out = output_after(s)
                if out is not None:
                    dve.wait_ge(o_hi_ready, out[0] + 1)
                    for d, b in output_pieces(out[0]):
                        ins = minus(d(b_lo), b, f32(d(b_hi)))
                    ins.then_inc(o_free, 1)
            rest_of_weights(dve, W_U + 4, 0)
            dve.wait_ge(wp_hi_ready, 1)
            minus(wp_lo[:], wp_raw[:], f32(wp_hi[:])).then_inc(wp_ready, 1)

            def mix(n):
                g = U_ORDER[n]
                w = 2 ** (g + 1)
                total, u = (sum_a, sum_b)[g % 2], u_all[:, g, :]
                dve.wait_ge(window_ready, n + 1)
                if n >= 1:
                    dve.wait_ge(diff_lo_ready, n)
                nc.vector.scalar_tensor_tensor(diff[:, w - 1:TP], total[:, NHIST + w - 1:NHIST + TP], 1.0 / w,
                                               u[:, NHIST + w - 1:NHIST + TP], mult, sub)
                nc.vector.scalar_tensor_tensor(diff[:, TP:T], total[:, U_S:U_S + TS], 1.0 / w,
                                               u[:, U_S:U_S + TS], mult, sub)
                c = slice(NHIST, NHIST + w - 1)
                after(nc.vector.tensor_tensor(diff[:, 0:w - 1], total[:, c], early_count[:, 0:w - 1], mult))
                nc.vector.tensor_tensor(diff[:, 0:w - 1], diff[:, 0:w - 1], u[:, c], sub).then_inc(diff_ready, 1)
                dve.wait_ge(diff_hi_ready, n + 1)
                minus(diff_lo[:, n % 2, :], diff[:], f32(diff_hi[:, n % 2, :])).then_inc(diff_lo_ready, 1)

            mix(0)
            mix(1)
            finish_u(2, 0)
            rest_of_weights(dve, W_U + 5, 1)
            finish_u(3, 1)
            mix(2)
            mix(3)
            for n, g in enumerate(U_ORDER):
                dve.wait_ge(pool_hi_ready, n + 1)
                scaled_minus(by_half(b_lo[:, g, :]), halves(ACC[n % 2]), pool_scale[:, g:g + 1],
                             by_half(f32(b_hi[:, g, :]))).then_inc(acc_free, 1)
            for q in range(4):
                n = len(MISCS) - 4 + q
                dve.wait_ge(misc_taken, n + 1)
                for c in range(2):
                    k = 2 * q + c
                    ins = scaled_minus(mem_lo[:, k, :], MISC[n % 4][:, c * MEM:c * MEM + MEM], g_mkv[:, k:k + 1],
                                       f32(mem_hi[:, k, :]))
                ins.then_inc(mem_gained, 1)

            dve.wait_ge(mem_stat_act, 1)
            nc.vector.reciprocal(stat[:, 20:22], stat[:, 18:20]).then_inc(mem_stat_dve, 1)

            def flat(x, k):
                return x[:, bass.ds(k, 1), :].rearrange("p k t -> p (k t)")

            def residual_steps(w0, first, gain, lo, hi):
                nc.vector.memset(square_sum[:], 0.0).then_inc(sum_ready, 1)
                with dve.Fori(0, KT // 2) as i:
                    for c in range(2):
                        k = i * 2 + c
                        rest_of_weights(dve, k + (w0 + 2), c)
                        dve.wait_ge(weight_used, k + (w0 + 1))
                        x = flat(x_t, k)
                        nc.vector.tensor_tensor(by_half(x), by_half(x), halves(ACC[c]), add).then_inc(acc_free, 1)
                        dve.wait_ge(acc_free, k + ((A_O if first == 0 else A_MO) + 1))
                        nc.vector.tensor_tensor(gained[:], x, gain[:, bass.ds(k, 1)].to_broadcast([P, T]),
                                                mult).then_inc(gained_ready, 1)
                        dve.wait_ge(act_hi_ready, k + (first + 1))
                        minus(flat(lo, k), gained[:], f32(flat(hi, k)))
                        dve.wait_ge(squared, k + (first + 1))
                        nc.vector.tensor_tensor(square_sum[:], square_sum[:], squares[:], add).then_inc(sum_ready, 1)

            def root(n):
                dve.wait_ge(root_done, n)
                nc.vector.reciprocal(inv_rms[:], inv_rms[:]).then_inc(rms_ready, 1)

            dve.wait_ge(misc_taken, len(MISCS))
            residual_steps(W_O, 0, g_xq, a_lo, a_hi)
            with dve.Fori(0, 2) as i:
                for c in range(2):
                    rest_of_weights(dve, i * 2 + (W_MK + 2 + c), c)
            root(1)
            with dve.Fori(0, 2) as i:
                for c in range(2):
                    rest_of_weights(dve, i * 2 + (W_MK + 6 + c), c)
            dve.wait_ge(rms_ready, 1)
            with dve.Fori(0, KT // 2) as i:
                for c in range(2):
                    k = i * 2 + c
                    rest_of_weights(dve, k + (W_MQ + 2), c)
                    dve.wait_ge(weight_used, k + (W_MQ + 1))
                    dve.wait_ge(mq_ready, k)
                    nc.vector.tensor_tensor(by_half(gained[:]), halves(ACC[c]), by_half(inv_rms[:]), mult).then_inc(acc_free, 1)
                    dve.wait_ge(mq_hi, k + 1)
                    scaled_minus(flat(b_lo, k), gained[:], MSCALE, f32(flat(b_hi, k))).then_inc(mq_ready, 1)

            def memory_keys(s):
                for q in range(4):
                    dve.wait_ge(mk_hi_done, 4 * s + q + 1)
                    k = slice(2 * q, 2 * q + 2)
                    minus(mk_lo[:, s, k, :], ACC[q // 2][:, q % 2].rearrange("p (k m) -> p k m", k=2),
                          f32(mk_hi[:, s, k, :])).then_inc(mk_ready, 1)

            memory_keys(0)
            with dve.Fori(0, 2) as i:
                for c in range(2):
                    rest_of_weights(dve, i * 2 + (W_MV + 2 + c), c)
            memory_keys(1)
            with dve.Fori(0, 2) as i:
                for c in range(2):
                    rest_of_weights(dve, i * 2 + (W_MV + 6 + c), c)
            for s in range(2):
                dve.wait_ge(kv_hi, s + 1)
                minus(mv_lo[:, s], kv_tok[:], f32(mv_hi[:, s])).then_inc(kv_lo, 1)

            for s in range(MH + 1 + 2):
                if s <= MH:
                    r = P if s < MH else TS
                    dve.wait_ge(ms_done, s + 1)
                    after(nc.vector.tensor_reduce(stat[0:r, 24:28], SC[0:r].rearrange("p b (q m) -> p (b q) m", q=2), X, ALU.max))
                    nc.vector.tensor_scalar(stat[0:r, 28:32], stat[0:r, 24:28], -1.0, None, mult).then_inc(ms_max, 1)
                if s >= 2:
                    m = s - 2
                    dve.wait_ge(mo_hi, m + 1)
                    minus(memory_output(a_lo, m), memory_bank(m), f32(memory_output(a_hi, m))).then_inc(mo_ready, 1)
                if 1 <= s <= MH + 1:
                    m = s - 1
                    w = TP if m < MH else MH * TS
                    dve.wait_ge(mt_hi, m + 1)
                    minus(mpt_lo[:, :, 0:w], OB[:, :, 0:w], f32(mpt_hi[:, :, 0:w])).then_inc(mt_ready, 1)
                if s <= MH:
                    dve.wait_ge(ms_exp, s + 1)
                    after(nc.vector.reciprocal(stat[0:r, 36:40], stat[0:r, 32:36]))
                    for q in range(4):
                        ins = nc.vector.tensor_scalar(mp[0:r, s % 2, q, :], mp[0:r, s % 2, q, :],
                                                      stat[0:r, 36 + q:37 + q], None, mult)
                    ins.then_inc(ms_prob, 1)

            residual_steps(W_MO, KT, g_ffn, b_lo, b_hi)
            nc.vector.memset(gate[:, 0:2], 0.0)
            nc.vector.memset(hidden[:], 0.0).then_inc(hidden_free, 1)
            root(2)
            dve.wait_ge(rms_ready, 2)
            for k, (f0, nf) in enumerate(CHUNKS):
                with dve.Fori(0, nf) as i:
                    f = i + f0
                    fc = bass.ds(f, 1)
                    rest_of_weights(dve, i * 2 + (W_UP[k] + 2), 0)
                    dve.wait_ge(weight_used, i * 2 + (W_UP[k] + 1))
                    acc = ACC[0]
                    nc.vector.tensor_tensor(gate[:, 2:2 + H], acc[:, 0, 0:H], inv_rms[:, 0:H], mult)
                    nc.vector.tensor_tensor(gate[:, 2 + H:2 + TP], acc[:, 1, 0:TP - H], inv_rms[:, H:TP], mult)
                    nc.vector.tensor_tensor(gate[:, GAP + 2:TE], acc[:, 1, TP - H:H], inv_rms[:, TP:T], mult).then_inc(acc_free, 1)
                    nc.vector.tensor_copy(gate[:, GAP:GAP + 2], conv_hist[:, :, fc].rearrange("p s f -> p (s f)"))
                    nc.vector.tensor_copy(par[:, 0:4], conv_par[:, :, fc].rearrange("p s f -> p (s f)")).then_inc(gate_ready, 1)
                    dve.wait_ge(gate_ready, i + (f0 + 1))
                    dve.wait_ge(acc_free, i * 2 + (A_UP[k] + 1))
                    for g in range(2):
                        c = (TP, TE - 2)[g]
                        nc.vector.tensor_copy(a_last[:, 2 * g:2 * g + 2, fc].rearrange("p s f -> p (s f)"), gate[:, c:c + 2])
                    dve.wait_ge(conv_first, i + (f0 + 1))
                    nc.vector.scalar_tensor_tensor(conv_b[:, 2:TE], gate[:, 1:TE - 1], par[:, 1:2], conv_a[:, 2:TE],
                                                   mult, add).then_inc(conv_second, 1)
                    dve.wait_ge(conv_second, i + (f0 + 1))
                    nc.vector.scalar_tensor_tensor(conv_a[:, 2:TE], gate[:, 0:TE - 2], par[:, 0:1], conv_b[:, 2:TE],
                                                   mult, add).then_inc(conv_ready, 1)
                    rest_of_weights(dve, i * 2 + (W_UP[k] + 3), 1)
                    dve.wait_ge(weight_used, i * 2 + (W_UP[k] + 2))
                    nc.vector.tensor_tensor(by_half(up_b[:]), halves(ACC[1]), by_half(inv_rms[:]), mult).then_inc(acc_free, 1)
                    dve.wait_ge(hidden_hi, f + 1)
                    minus(flat(a_lo, i), hidden[:], f32(flat(a_hi, i))).then_inc(hidden_free, 1)

                def down(k_, n, c):
                    dve.wait_ge(weight_used, n + 1)
                    x = flat(x_t, k_)
                    nc.vector.tensor_tensor(by_half(x), by_half(x), halves(ACC[c]), add).then_inc(acc_free, 1)

                whole = KT // 2 - (k == 2)
                with dve.Fori(0, whole) as i:
                    for c in range(2):
                        rest_of_weights(dve, i * 2 + (W_DOWN[k] + 2 + c), c)
                        down(i * 2 + c, i * 2 + (W_DOWN[k] + c), c)
                if k == 2:
                    for c in range(2):
                        down(KT - 2 + c, W_DOWN[k] + KT - 2 + c, c)
            dve.wait_ge(g_final_landed, 16)
            for t in range(NT + 1):
                r = P if t < NT else TS
                dve.wait_ge(y_root, t + 1)
                after(nc.vector.reciprocal(stat[0:r, 56 + t:57 + t], stat[0:r, 48 + t:49 + t]))
                nc.vector.scalar_tensor_tensor(y_tok[0:r, t, :].rearrange("p (b c) -> p b c", b=2), final_bank(t)[0:r],
                                               stat[0:r, 56 + t:57 + t], g_final[0:r, :].rearrange("p (b c) -> p b c", b=2),
                                               mult, mult).then_inc(y_ready, 1)

        @block.tensor
        def _(pe):
            mm, turn = nc.tensor.matmul, nc.tensor.transpose
            pe.wait_ge(consts_ready, 13)
            pe.wait_ge(rows_landed, 16 * 9)
            bank = OB[:, 1]
            turn(bank[:, 0:NG], rows_in[0:NG, 0, :], ident[0:NG, 0:NG])
            turn(bank[:, 64:64 + 4 * NF], rows_in[0:4 * NF, 1, :], ident[0:4 * NF, 0:4 * NF])
            turn(bank[:, 192:192 + 2 * NF], rows_in[0:2 * NF, 2, :], ident[0:2 * NF, 0:2 * NF])
            for g in range(GROUPS):
                ins = turn(bank[:, 256 + 16 * g:256 + 16 * g + NHIST], hist_tok[0:NHIST, g * P:g * P + P],
                           ident[0:NHIST, 0:NHIST])
            ins.then_inc(cols_turned, 1)
            pe.wait_ge(xr_ready, NT + 1)
            pe.wait_ge(cols_ready, 4)
            for k in range(KT):
                ins = turn(bank[:, k * TS:k * TS + TS], xr_tok[0:TS, NT, k * P:k * P + P], ident[0:TS, 0:TS])
            ins.then_inc(hs_turned, 1)

            def h_turn(k):
                if k >= 2:
                    pe.wait_ge(h_lo_ready, k - 1)
                b = (SC[:, 1], OB[:, 0])[k % 2]
                for t in range(NT):
                    ins = turn(b[:, t * P:t * P + P], xr_tok[:, t, k * P:k * P + P], ident[:])
                ins.then_inc(h_turned, 1)

            def values(k):
                n, sub = W_V + k // 2, k % 2
                pe.wait_ge(weight_lo_ready, n + 1)
                pe.wait_ge(h_lo_ready, min(k + 2, KT))
                pe.wait_ge(hs_lo_ready, 1)
                c = slice(sub * DFOX, sub * DFOX + DFOX)
                for t in range(NT + 1):
                    b = ACC[t // 2][:, t % 2] if t < NT else SC[:, 0]
                    for x, w in ((0, w_hi), (0, w_lo), (1, w_hi)):
                        ins = mm(b, flat_a[x][:, k * T + t * P:k * T + t * P + P], w[n % 2][:, c],
                                 start=(k == 0 and x == 0 and w is w_hi), stop=(k == KT - 1 and x == 1))
                if sub == 1:
                    ins.then_inc(weight_used, 1)

            h_turn(0)
            h_turn(1)
            for k in range(KT):
                if k + 2 < KT:
                    h_turn(k + 2)
                values(k)
            pe.wait_ge(wf_ready, 1)
            pe.wait_ge(h_lo_ready, KT)
            for k in range(KT):
                for w, x in ((wf_hi, a_hi), (wf_hi, a_lo), (wf_lo, a_hi)):
                    for h in range(2):
                        ins = mm(OB[:, h, 0:H], w[:, k, :], x[:, k, h * H:h * H + H],
                                 start=(k == 0 and w is wf_hi and x is a_hi), stop=(k == KT - 1 and w is wf_lo))
            ins.then_inc(gate_done, 1)
            pe.wait_ge(v_copied, NT + 1)
            pe.wait_ge(v_free, NT + 1)
            for c in range(CT):
                ins = turn(SC[0:HEADS, c // 4, c % 4 * P:c % 4 * P + P], cl_tok[:, c, :], ident[:])
            ins.then_inc(gate_done, 1)

            for n in (W_QK, W_QK + 1):
                pe.wait_ge(weight_lo_ready, n + 1)
                if n > W_QK:
                    pe.wait_ge(acc_free, A_QK + 1)
                project(n % 2, a_hi, a_lo, ACC[0], range(KT), KT)

            for s in range(STEPS):
                j, e = divmod(s, ENTRIES)
                if s < N_ENTRIES:
                    b = j % 2
                    if s >= 2:
                        pe.wait_ge(scores_taken, s - 1)
                    else:
                        pe.wait_ge(gate_dve, 3)
                    if e == 0:
                        pe.wait_ge(acc_free, A_QK + 2 * j + 2)
                        pe.wait_ge(masks_split, 4)
                    bank, w = SC[:, s % 2], keys_of(e)
                    if e < 2 * NT:
                        h, t = e // NT, e % NT
                        r, c = slice(h * DH, h * DH + DH), slice(t * P, t * P + P)
                        for q, kk in ((q_hi, k_hi), (q_hi, k_lo), (q_lo, k_hi)):
                            mm(bank[:, 0:w], q[r, b, c], kk[r, b, 0:w], start=(q is q_hi and kk is k_hi), stop=False)
                        ins = mm(bank[:, c], ident_r[:], causal_r[:], start=False, stop=True)
                    elif e < ENTRIES - 1:
                        c = slice((e - 2 * NT) * 512, (e - 2 * NT) * 512 + 512)
                        pe.wait_ge(turn_ready, TURN[("K", j, 1)] + 1)
                        for q, kk in ((qs_hi, kc_hi), (qs_hi, kc_lo), (qs_lo, kc_hi)):
                            ins = mm(bank, q[:, b, :], kk[:, c], start=(q is qs_hi and kk is kc_hi), stop=(q is qs_lo))
                    else:
                        for q, kk in ((qs_hi, k_hi), (qs_hi, k_lo), (qs_lo, k_hi)):
                            mm(bank[:, 0:TS], q[:, b, :], kk[:, b, TP:T], start=(q is qs_hi and kk is k_hi), stop=False)
                        ins = mm(bank[:, 0:TS], ident_r[:], causal_s[:], start=False, stop=True)
                    ins.then_inc(scores_done, 1)
                if j < PAIRS and e in FILL:
                    which, tiles = FILL[e]
                    n = W_QK + 2 * (j + 1) + which
                    if tiles[0] == 0:
                        pe.wait_ge(weight_lo_ready, n + 1)
                        pe.wait_ge(acc_free, A_QK + 2 * (j + 1) + which)
                    project(n % 2, a_hi, a_lo, ACC[0], tiles, KT)
                for t in turns_of(s):
                    what = TURNS[t]
                    if t >= 2:
                        pe.wait_ge(turn_ready, t - 1)
                    if what[0] == "K":
                        pe.wait_ge(cache_k_landed, 16 * (what[1] + 1))
                        for c in range(4):
                            ins = turn(TB[t % 2][:, c * P:c * P + P], kc_raw[:, what[2] * 4 + c, :], ident[:])
                    else:
                        e_t = what[1] % ENTRIES
                        pe.wait_ge(prob_ready, probs_done(what[1]))
                        if e_t < 2 * NT:
                            p = prob_p[:, prompt_slot(what[1]), :]
                            n_t = e_t % NT + 1
                        else:
                            p = prob_s[:, (e_t - 2 * NT) * 512:]
                            n_t = 4 if e_t < ENTRIES - 1 else 0
                        for c in range(n_t):
                            ins = turn(TB[t % 2][:, c * P:c * P + P], p[:, c * P:c * P + P], ident[:])
                        if n_t == 0:
                            ins = turn(TB[t % 2][0:TS, 0:P], p[:, 0:TS], ident[:])
                    ins.then_inc(turn_done, 1)
                g = s - LAG - 1
                if 0 <= g < N_ENTRIES:
                    jg, eg = divmod(g, ENTRIES)
                    t = TURN[("P", g)]
                    n, bank = output_of(g)
                    pe.wait_ge(turn_ready, t + 1)
                    if eg % NT == 0 and output_bank_free(n) is not None:
                        pe.wait_ge(o_free, output_bank_free(n))
                    feats = slice(jg * P, jg * P + P)
                    if eg < 2 * NT:
                        out = bank[:, eg % NT * P:eg % NT * P + P]
                        n_k, n_0, n_all = eg % NT + 1, 0, eg % NT + 1
                    else:
                        out = bank[:, 0:P]
                        n_k, n_0, n_all = (4 if eg < ENTRIES - 1 else 1), 4 * (eg - 2 * NT), CT + 1
                        pe.wait_ge(vc_ready, jg + 1)
                    for c in range(n_k):
                        at_c = n_0 + c
                        for vx, px in ((0, pt_hi), (0, pt_lo), (1, pt_hi)):
                            if eg < 2 * NT:
                                v, pp = (v_hi, v_lo)[vx][:, c, feats], px[:, t % 2, c * P:c * P + P]
                            elif eg < ENTRIES - 1:
                                v, pp = (vc_hi, vc_lo)[vx][:, at_c, :], px[:, t % 2, c * P:c * P + P]
                            else:
                                v, pp = (own_hi, own_lo)[vx][:, feats], px[0:TS, t % 2, 0:P]
                            ins = mm(out, v, pp, start=(at_c == 0 and vx == 0 and px is pt_hi),
                                     stop=(at_c == n_all - 1 and vx == 1))
                    ins.then_inc(pv_done, 1)
            for n in (2, 3):
                pe.wait_ge(weight_lo_ready, W_U + n + 1)
                pe.wait_ge(acc_free, A_U + 2)
                pe.wait_ge(turn_ready, len(TURNS))
                project(n % 2, a_hi, a_lo, ACC[n % 2], range(KT), KT)
            pe.wait_ge(wp_ready, 1)
            for n, g in enumerate(U_ORDER):
                pe.wait_ge(diff_lo_ready, n + 1)
                pe.wait_ge(acc_free, (A_U + 3, A_U + 4, A_U + 5, A_U + 6)[n])
                for w, x in ((wp_hi, diff_hi), (wp_hi, diff_lo), (wp_lo, diff_hi)):
                    for h in range(2):
                        ins = mm(ACC[n % 2][:, h, 0:H], w[:, g, :], x[:, n % 2, h * H:h * H + H],
                                 start=(w is wp_hi and x is diff_hi), stop=(w is wp_lo))
                ins.then_inc(pool_done, 1)
            pe.wait_ge(scores_taken, N_ENTRIES)
            pe.wait_ge(o_free, OUTPUTS * PAIRS)
            for n, (kind, m) in enumerate(MISCS):
                bank = MISC[n % 4]
                if n >= 4:
                    pe.wait_ge(misc_taken, n - 3)
                if kind == "k":
                    r = P if m < NT else TS
                    for j in range(PAIRS):
                        ins = turn(bank[0:r, j * P:j * P + P], k_new[:, j, m * P:m * P + r], ident[:])
                elif kind == "u":
                    end = (NHIST + TP, U_S + TS)[m]
                    for g in range(GROUPS):
                        ins = turn(bank[0:NHIST, g * P:g * P + P], u_all[:, g, end - NHIST:end], ident[:])
                elif kind == "f":
                    for t in range(NT + 1):
                        r = P if t < NT else TS
                        ins = turn(bank[0:r, t * HEADS:t * HEADS + HEADS], logf[:, t * P:t * P + r], ident[0:HEADS, 0:HEADS])
                elif kind == "x":
                    pe.wait_ge(misc_landed, 16 * (NT + 1))
                    for t in range(NT):
                        ins = turn(bank[:, t * P:t * P + P], x_again[:, t, m * P:m * P + P], ident[:])
                elif kind == "xs":
                    for k in range(KT):
                        ins = turn(bank[:, k * TS:k * TS + TS], x_again[0:TS, NT, k * P:k * P + P], ident[0:TS, 0:TS])
                else:
                    pe.wait_ge(mem_landed, 16)
                    for c in range(2):
                        for t in range(MT):
                            ins = turn(bank[:, c * MEM + t * P:c * MEM + t * P + P],
                                       mem_tok[:, t, (2 * m + c) * P:(2 * m + c) * P + P], ident[:])
                ins.then_inc(misc_turned, 1)

            def mean(n, value, bank):
                pe.wait_ge(sum_ready, value)
                for h in range(2):
                    ins = mm(bank[:, h, 0:H], mean_w[:], square_sum[:, h * H:h * H + H], start=True, stop=True)
                ins.then_inc(mean_done, 1)

            def project_all(w0, a0, x_hi, x_lo, total=KT, rounds=KT // 2):
                with pe.Fori(0, rounds) as i:
                    for c in range(2):
                        pe.wait_ge(weight_lo_ready, i * 2 + (w0 + c + 1))
                        pe.wait_ge(acc_free, i * 2 + (a0 + c - 1))
                        project(c, x_hi, x_lo, ACC[c], range(total), total)

            pe.wait_ge(acc_free, A_O)
            project_all(W_O, A_O, b_hi, b_lo)

            def memory_tile(n, slot, k, first, last):
                pe.wait_ge(weight_lo_ready, n + 1)
                for t in range(MT):
                    for h in range(2):
                        for x, w in ((mem_hi, w_hi), (mem_lo, w_hi), (mem_hi, w_lo)):
                            ins = mm((SC, OB)[t][:, h], x[:, k, t * P:t * P + P], w[slot][:, h * 512:h * 512 + 512],
                                     start=(first and x is mem_hi and w is w_hi), stop=(last and w is w_lo))
                ins.then_inc(weight_used, 1)

            pe.wait_ge(mem_gained, 4)
            for k in range(KT // 2):
                memory_tile(W_MK + k, k % 2, k, k == 0, False)
            pe.wait_ge(acc_free, A_O + KT)
            mean(1, KT + 1, ACC[0])
            for k in range(KT // 2, KT):
                memory_tile(W_MK + k, k % 2, k, False, k == KT - 1)
            pe.wait_ge(root_done, 1)
            project_all(W_MQ, A_MQ, a_hi, a_lo)

            def memory_keys(s):
                pe.wait_ge(acc_free, A_MQ + KT)
                if s == 0:
                    pe.wait_ge(kv_out, 2)
                else:
                    pe.wait_ge(ck_landed, 16)
                    pe.wait_ge(mk_ready, 4)
                for q in range(4):
                    for c in range(2):
                        for t in range(MT):
                            ins = turn(ACC[q // 2][:, q % 2, c * MEM + t * P:c * MEM + t * P + P],
                                       kv_tok[:, t, (2 * q + c) * P:(2 * q + c) * P + P], ident[:])
                    ins.then_inc(mk_turned, 1)

            memory_keys(0)
            for k in range(KT // 2):
                memory_tile(W_MV + k, k % 2, k, k == 0, False)
            memory_keys(1)
            for k in range(KT // 2, KT):
                memory_tile(W_MV + k, k % 2, k, False, k == KT - 1)

            pe.wait_ge(kv_out, 4)
            pe.wait_ge(mq_ready, KT)
            pe.wait_ge(mk_ready, 8)
            for s in range(MH + 1 + 2):
                if s <= MH:
                    if s >= 1:
                        pe.wait_ge(ms_exp, s)
                    for q in range(4):
                        out = SC[:, q // 2, q % 2 * MEM:q % 2 * MEM + MEM]
                        for f in range(2):
                            k = 2 * (s if s < MH else q) + f
                            col = k * T + (q * P if s < MH else TP)
                            for x, kk in ((0, mk_hi), (0, mk_lo), (1, mk_hi)):
                                ins = mm(out, flat_b[x][:, col:col + P], kk[:, s // MH, k, :],
                                         start=(f == 0 and x == 0 and kk is mk_hi), stop=(f == 1 and x == 1))
                    ins.then_inc(ms_done, 1)
                if s >= 2:
                    m = s - 2
                    pe.wait_ge(mt_ready, m + 1)
                    pe.wait_ge(kv_lo, 1 if m < MH else 2)
                    if m >= 2:
                        pe.wait_ge(mo_ready, m - 1)
                    for f in range(2 if m < MH else 2 * MH):
                        if m < MH:
                            out, c, k = ACC[m % 2][:, f], slice(0, TP), 2 * m + f
                        else:
                            out, k = ACC[0][:, 0, f * TS:f * TS + TS], f
                            c = slice(f // 2 * TS, f // 2 * TS + TS)
                        for b in range(MT):
                            for v, pp in ((mv_hi, mpt_hi), (mv_hi, mpt_lo), (mv_lo, mpt_hi)):
                                ins = mm(out, v[:, m // MH, b, k * P:k * P + P], pp[:, b, c],
                                         start=(b == 0 and v is mv_hi and pp is mpt_hi), stop=(b == MT - 1 and v is mv_lo))
                    ins.then_inc(mo_done, 1)
                if 1 <= s <= MH + 1:
                    m = s - 1
                    pe.wait_ge(ms_prob, m + 1)
                    if m >= 1:
                        pe.wait_ge(mt_ready, m)
                    for b in range(MT):
                        for q in range(4):
                            if m < MH:
                                ins = turn(OB[:, b, q * P:q * P + P], mp[:, m % 2, q, b * P:b * P + P], ident[:])
                            else:
                                ins = turn(OB[:, b, q * TS:q * TS + TS], mp[0:TS, m % 2, q, b * P:b * P + P], ident[0:TS, 0:TS])
                    ins.then_inc(mt_done, 1)
            pe.wait_ge(mo_ready, MH + 1)
            project_all(W_MO, A_MO, a_hi, a_lo)
            mean(2, 2 * KT + 2, SC)
            for k, (f0, nf) in enumerate(CHUNKS):
                project_all(W_UP[k], A_UP[k], b_hi, b_lo, rounds=nf)
                pe.wait_ge(hidden_free, f0 + nf + 1)
                project_all(W_DOWN[k], A_DOWN[k], a_hi, a_lo, total=nf)
            turn(MISC[0][0:4 * NF, 0:P], a_last[:].rearrange("p s f -> p (s f)"), ident[:]).then_inc(conv_turned, 1)
            pe.wait_ge(acc_free, a_all)
            for t in range(NT + 1):
                r = P if t < NT else TS
                if t == 1:
                    pe.wait_ge(conv_tok_ready, 1)
                if t == NT:
                    pe.wait_ge(y_ready, 1)
                for k in range(KT):
                    ins = turn(final_bank(t)[0:r, k // 4, k % 4 * P:k % 4 * P + P], x_t[:, k, t * P:t * P + r], ident[:])
                ins.then_inc(y_turned, 1)


_INS = ['x_prompt', 'x_sample', 'cache_fox_k', 'cache_fox_v', 'cache_fox_logf', 'state_pool', 'state_ffn_conv',
        'cache_mem_k', 'cache_mem_v', 'mem_prompt', 'g_mix', 'w_in', 'b_f', 'w_pool', 'pool_scale', 'w_o',
        'g_xq', 'g_mkv', 'w_mq', 'w_mk', 'w_mv', 'w_mo', 'g_ffn', 'w_up', 'conv_w', 'conv_b', 'w_down', 'g_final']


def declare(nc, shapes):
    a = {n: nc.dram_tensor(f"in_{n}", shapes[n], F32, kind="ExternalInput").ap() for n in _INS}
    depth, batch, past, heads, dh = shapes['cache_fox_k']
    _, tp, d = shapes['x_prompt']
    ts = shapes['x_sample'][1]
    mem = shapes['cache_mem_k'][2:]
    outs = [('y_prompt', (batch, tp, d)), ('y_sample', (batch, ts, d)),
            ('fox_k_prompt', (depth, batch, tp, heads, dh)), ('fox_v_prompt', (depth, batch, tp, heads, dh)),
            ('fox_logf_prompt', (depth, batch, tp, heads)), ('pool_state_prompt', shapes['state_pool']),
            ('conv_state_prompt', shapes['state_ffn_conv']), ('mem_k_prompt', (depth, batch) + tuple(mem)),
            ('mem_v_prompt', (depth, batch) + tuple(mem)),
            ('fox_k_sample', (depth, batch, ts, heads, dh)), ('fox_v_sample', (depth, batch, ts, heads, dh)),
            ('fox_logf_sample', (depth, batch, ts, heads)), ('pool_state_sample', shapes['state_pool']),
            ('conv_state_sample', shapes['state_ffn_conv'])]
    o = {n: nc.dram_tensor(f"out_{n}", s, F32, kind="ExternalOutput").ap() for n, s in outs}
    build(nc, a, o)
    return [n for n, _ in outs]


def kernel(**inputs):
    import concourse.bacc as bacc
    import numpy as np
    from concourse.bass_utils import run_bass_kernel_spmd as run

    arrays = {n: np.ascontiguousarray(inputs[n]) for n in _INS}
    nc = bacc.Bacc("TRN2", target_bir_lowering=False, num_devices=1, dynamic_dma_scratch_size=DMA_SCRATCH)
    names = declare(nc, {n: x.shape for n, x in arrays.items()})
    r = run(nc, [{f"in_{n}": x for n, x in arrays.items()}], core_ids=[0])
    return tuple(r.results[0][f"out_{n}"] for n in names)
```

```python
from contextlib import ExitStack

import concourse.bass as bass
from concourse import mybir
from concourse.alu_op_type import AluOpType as ALU

ACT = mybir.ActivationFunctionType
F32 = mybir.dt.float32
F32R = mybir.dt.float32r
X = mybir.AxisListType.X
P = 128
EPS = 1e-6
MASKED = -1e30
DMA_SCRATCH = 3072


class Tally:

    def __init__(self, sem):
        self.sem, self.base, self.n, self.i, self.per = sem, 0, 0, None, 0

    @property
    def now(self):
        return self.base + self.n if self.i is None else self.i * self.per + (self.base + self.n)

    def inc(self, instruction):
        instruction.then_inc(self.sem, 1)
        self.n += 1

    def enter(self, i, per):
        self.base, self.n, self.i, self.per = self.base + self.n, 0, i, per

    def leave(self, rounds):
        assert self.n == self.per, (self.n, self.per)
        self.base, self.n, self.i = self.base + rounds * self.per, 0, None


def build(nc, a, o):
    TP, D = a["x_prompt"].shape[1:]
    TS = a["x_sample"].shape[1]
    T = TP + TS
    H = T // 2
    KT = D // P
    PAST, HEADS, DH = a["cache_fox_k"].shape[2:]
    DFOX = HEADS * DH
    PAIRS = HEADS // 2
    NHIST, DPOOL = a["state_pool"].shape[2:]
    GROUPS = DPOOL // P
    DFF = a["w_down"].shape[1]
    NF = DFF // P
    MEM, MH, MD = a["cache_mem_k"].shape[2:]
    MT = MEM // P
    NT = TP // P
    CT = PAST // P
    KEYS = PAST + TS
    QSCALE = float(DH) ** -0.5
    MSCALE = float(MD) ** -0.5
    D_IN = DPOOL + 3 * DFOX + HEADS
    assert 2 * DH == P and MD == 2 * P and TS == DH and KT == 8 and NT == 4 and MT == 2

    CHUNKS = [(0, 8), (8, 8), (16, 6)]
    assert sum(c[1] for c in CHUNKS) == NF
    W_V, W_QK, W_U, W_O, W_MK, W_MQ, W_MV, W_MO = 0, 4, 12, 16, 24, 32, 40, 48
    A_QK, A_U, A_POOL, A_O, A_MQ, A_MO = 0, 8, 12, 16, 24, 32
    W_UP, W_DOWN, A_UP, A_DOWN = [], [], [], []
    w_all, a_all = 56, 40
    for _, nf in CHUNKS:
        W_UP.append(w_all)
        W_DOWN.append(w_all + 2 * nf)
        A_UP.append(a_all)
        A_DOWN.append(a_all + 2 * nf)
        w_all += 2 * nf + KT
        a_all += 2 * nf + KT

    ENTRIES, LAG = 2 * NT + 3, 3
    N_ENTRIES = PAIRS * ENTRIES
    TURNS = []
    for s in range(N_ENTRIES + LAG):
        j, e = divmod(s, ENTRIES)
        if j < PAIRS and e in (2, 5):
            TURNS.append(("K", j, 0 if e == 2 else 1))
        if s >= LAG:
            TURNS.append(("P", s - LAG))
    TURN = {what: n for n, what in enumerate(TURNS)}
    FILL = {0: (0, [0, 1]), 1: (0, [2, 3]), 2: (0, [4]), 3: (0, [5]), 4: (0, [6, 7]),
            6: (1, [0, 1, 2]), 7: (1, [3]), 8: (1, [4, 5]), 9: (1, [6, 7])}

    decay_p_dram = nc.dram_tensor("decay_prompt", (HEADS, TP), F32, kind="Internal").ap()
    decay_s_dram = nc.dram_tensor("decay_sample", (HEADS, KEYS), F32, kind="Internal").ap()

    ctx = ExitStack()
    with ctx:
        slab_bytes = (nc.sbuf_bytes_remaining - 96) // 32 * 32
        slab_at = (nc.sbuf_base + 31) // 32 * 32
        ctx.enter_context(nc.sbuf_tensor("slab", [P, slab_bytes // 4], F32))
        at = {}
        here = [0]

        def place(name, shape, dtype=F32):
            size = 4
            for s in shape[1:]:
                size *= s
            at[name] = here[0]
            here[0] += (size + 31) // 32 * 32
            assert here[0] <= slab_bytes, (name, here[0], slab_bytes)
            return nc.alloc_sbuf_tensor_at(name, shape, dtype, offset=slab_at + at[name])

        w_raw = [place(f"w_raw{s}", [P, D]) for s in range(2)]
        w_hi = [place(f"w_hi{s}", [P, D], F32R) for s in range(2)]
        w_lo = [place(f"w_lo{s}", [P, D], F32R) for s in range(2)]
        flat_a = [place(f"a_{s}", [P, KT * T + P - TS], F32R) for s in ("hi", "lo")]
        a_hi, a_lo = (x[:, 0:KT * T].rearrange("p (k t) -> p k t", k=KT) for x in flat_a)
        flat_b = [place(f"b_{s}", [P, KT * T + P - TS], F32R) for s in ("hi", "lo")]
        b_hi, b_lo = (x[:, 0:KT * T].rearrange("p (k t) -> p k t", k=KT) for x in flat_b)
        ident = place("ident", [P, P])
        ident_r = place("ident_r", [P, P], F32R)
        causal_r = place("causal_r", [P, P], F32R)
        causal_s = place("causal_s", [P, DH], F32R)
        mean_w = place("mean_w", [P, P])
        eps = place("eps", [P, 1])
        one = place("one", [P, 1])
        NG = 4 * KT + GROUPS
        gains = place("gains", [P, NG])
        g_mix, g_xq, g_mkv, g_ffn = (gains[:, KT * k:KT * k + KT] for k in range(4))
        pool_scale = gains[:, 4 * KT:NG]
        conv_par = place("conv_par", [P, 4, NF])
        conv_hist = place("conv_hist", [P, 2, NF])
        b_f = place("b_f", [HEADS, 1])
        inv_rms = place("inv_rms", [P, T])
        logf = place("logf", [HEADS, T])
        a_last = place("a_last", [P, 4, NF])
        early_count = place("early_count", [P, 16])
        stat = place("stat", [P, 64])
        phase = here[0]

        v_hi = place("v_hi", [P, NT, DFOX], F32R)
        v_lo = place("v_lo", [P, NT, DFOX], F32R)
        own_hi = place("own_hi", [TS, DFOX], F32R)
        own_lo = place("own_lo", [TS, DFOX], F32R)
        q_hi = place("q_hi", [P, 2, TP], F32R)
        q_lo = place("q_lo", [P, 2, TP], F32R)
        k_hi = place("k_hi", [P, 2, T], F32R)
        k_lo = place("k_lo", [P, 2, T], F32R)
        qs_hi = place("qs_hi", [P, 2, P], F32R)
        qs_lo = place("qs_lo", [P, 2, P], F32R)
        k_new = place("k_new", [P, PAIRS, T])
        decay_p = place("decay_p", [P, 2, 2, TP])
        decay_s = place("decay_s", [P, KEYS])
        prob_p = place("prob_p", [P, 4, TP])
        pt_hi = place("pt_hi", [P, 2, TP], F32R)
        pt_lo = place("pt_lo", [P, 2, TP], F32R)
        vc_hi = place("vc_hi", [P, CT, P], F32R)
        vc_lo = place("vc_lo", [P, CT, P], F32R)
        fox_stat = place("fox_stat", [P, N_ENTRIES, 4])
        prob_s = place("prob_s", [P, KEYS])
        kc_hi = place("kc_hi", [P, PAST], F32R)
        kc_lo = place("kc_lo", [P, PAST], F32R)
        kc_raw = place("kc_raw", [P, CT, P])
        vc_raw = place("vc_raw", [P, CT, P])
        u_all = place("u_all", [P, GROUPS, NHIST + TP + NHIST + TS])
        U_S = NHIST + TP + NHIST
        here[0] = at["decay_p"]
        x_tok = place("x_tok", [P, NT + 1, D])
        xr_tok = place("xr_tok", [P, NT + 1, D])
        square = place("square", [P, D])
        x_gained_s = place("x_gained_s", [P, KT, TS])
        wf_raw = place("wf_raw", [P, KT, HEADS])
        wf_hi = place("wf_hi", [P, KT, P], F32R)
        wf_lo = place("wf_lo", [P, KT, P], F32R)
        cl_tok = place("cl_tok", [P, CT, HEADS])
        rows_in = place("rows_in", [P, 3, P])
        hist_tok = place("hist_tok", [16, DPOOL])
        causal = place("causal", [P, P])
        here[0] = at["prob_p"]
        v_out = place("v_out", [P, NT + 1, DFOX])
        z = place("z", [HEADS, T])
        z_abs = place("z_abs", [HEADS, T])
        z_min = place("z_min", [HEADS, T])
        log_s = place("log_s", [HEADS, KEYS])
        ones_row = place("ones_row", [HEADS, KEYS])
        cum_p = place("cum_p", [HEADS, TP])
        cum_s = place("cum_s", [HEADS, KEYS])
        assert here[0] <= at["wf_raw"]
        here[0] = phase
        x_t = place("x_t", [P, KT, T])
        mem_at = here[0]
        mem_hi = place("mem_hi", [P, KT, MEM], F32R)
        mem_lo = place("mem_lo", [P, KT, MEM], F32R)
        here[0] = mem_at
        diff_hi = place("diff_hi", [P, 2, T], F32R)
        diff_lo = place("diff_lo", [P, 2, T], F32R)
        here[0] = at["mem_lo"] + 4 * KT * MEM
        gate_tok = place("gate_tok", [P, NT + 1, HEADS])
        assert here[0] <= at["k_new"]
        here[0] = at["decay_p"]
        sum_a = place("sum_a", [P, U_S + TS])
        sum_b = place("sum_b", [P, U_S + TS])
        diff = place("diff", [P, 2, T])
        pool_tok = place("pool_tok", [NHIST, 2, DPOOL])
        assert here[0] <= at["pt_hi"]
        here[0] = at["decay_p"]
        mem_squares = place("mem_squares", [P, MT, D])
        assert here[0] <= at["pool_tok"]
        here[0] = at["pt_hi"]
        wp_raw = place("wp_raw", [P, GROUPS, P])
        wp_hi = place("wp_hi", [P, GROUPS, P], F32R)
        wp_lo = place("wp_lo", [P, GROUPS, P], F32R)
        k_tok = place("k_tok", [P, NT + 1, DFOX])
        assert here[0] <= at["prob_s"]
        here[0] = at["prob_s"]
        x_again = place("x_again", [P, NT + 1, D])
        assert here[0] <= at["u_all"]
        here[0] = slab_bytes - 3 * 4 * T - 96
        gained = place("gained", [P, T])
        squares = place("squares", [P, T])
        square_sum = place("square_sum", [P, T])
        tail = at["gained"]
        here[0] = at["a_hi"]
        mem_tok = place("mem_tok", [P, MT, D])
        here[0] = mem_at
        mp = place("mp", [P, 2, 4, MEM])
        mpt_hi = place("mpt_hi", [P, MT, TP], F32R)
        mpt_lo = place("mpt_lo", [P, MT, TP], F32R)
        here[0] = mem_at + 2 * 4 * KT * MEM
        kv_tok = place("kv_tok", [P, MT, D])
        mk_hi = place("mk_hi", [P, 2, KT, MEM], F32R)
        mk_lo = place("mk_lo", [P, 2, KT, MEM], F32R)
        mv_hi = place("mv_hi", [P, 2, MT, D], F32R)
        mv_lo = place("mv_lo", [P, 2, MT, D], F32R)
        assert here[0] <= tail, (here[0], tail)
        here[0] = mem_at
        GAP = TP + 2
        TE = GAP + 2 + TS
        gate = place("gate", [P, TE])
        up_b = place("up_b", [P, T])
        conv_a = place("conv_a", [P, TE])
        conv_b = place("conv_b", [P, TE])
        silu = place("silu", [P, TE])
        hidden = place("hidden", [P, T])
        par = place("par", [P, 6])
        conv_tok = place("conv_tok", [4 * NF, P])
        y_tok = place("y_tok", [P, NT + 1, D])
        y_junk = place("y_junk", [P, D])
        g_final = place("g_final", [P, D])

        ps = [ctx.enter_context(nc.psum_tensor(f"ps{n}", [P, 2, 512], F32)) for n in range(4)]
        ACC, SC, OB = ps[0:2], ps[2], ps[3]
        TB = [ps[1][:, 0], ps[1][:, 1]]
        MISC = [ps[2][:, 0], ps[2][:, 1], ps[3][:, 0], ps[3][:, 1]]

        def sem(name):
            return ctx.enter_context(nc.semaphore(name))

        weight_landed = [sem("weight_landed0"), sem("weight_landed1")]
        weight_hi_ready, weight_lo_ready, weight_used = sem("weight_hi_ready"), sem("weight_lo_ready"), sem("weight_used")
        acc_free = sem("acc_free")
        x_landed = [sem(f"x_landed{t}") for t in range(NT + 1)]
        g_mix_landed = sem("g_mix_landed")
        rows_landed, more_rows_landed, small_landed = sem("rows_landed"), sem("more_rows_landed"), sem("small_landed")
        early_ready = sem("early_ready")
        consts_ready, masks_ready, masks_split = sem("consts_ready"), sem("masks_ready"), sem("masks_split")
        x_squared, x_rms, xr_ready = sem("x_squared"), sem("x_rms"), sem("xr_ready")
        cols_turned, cols_ready = sem("cols_turned"), sem("cols_ready")
        hs_turned, hs_gained, h_turned, h_hi_ready, h_lo_ready = (
            sem("hs_turned"), sem("hs_gained"), sem("h_turned"), sem("h_hi_ready"), sem("h_lo_ready"))
        hs_hi_ready = sem("hs_hi_ready")
        v_copied, v_free = sem("v_copied"), sem("v_free")
        window_ready, hs_lo_ready = sem("window_ready"), sem("hs_lo_ready")
        wf_hi_ready, wf_ready = sem("wf_hi_ready"), sem("wf_ready")
        gate_done, gate_act, gate_dve = sem("gate_done"), sem("gate_act"), sem("gate_dve")
        cum_ready, cum_stored = sem("cum_ready"), sem("cum_stored")
        decay_landed = [sem("decay_landed0"), sem("decay_landed1")]
        decay_s_landed = sem("decay_s_landed")
        cache_k_landed, cache_v_landed = sem("cache_k_landed"), sem("cache_v_landed")
        qk_hi_ready = sem("qk_hi_ready")
        scores_done, scores_taken = sem("scores_done"), sem("scores_taken")
        exp_done, prob_ready = sem("exp_done"), sem("prob_ready")
        turn_done, turn_hi_ready, turn_ready = sem("turn_done"), sem("turn_hi_ready"), sem("turn_ready")
        pv_done, o_hi_ready, o_free = sem("pv_done"), sem("o_hi_ready"), sem("o_free")
        vc_hi_ready, vc_ready = sem("vc_hi_ready"), sem("vc_ready")
        misc_landed, mem_landed = sem("misc_landed"), sem("mem_landed")
        wp_landed, wp_hi_ready, wp_ready = sem("wp_landed"), sem("wp_hi_ready"), sem("wp_ready")
        diff_ready, diff_hi_ready, diff_lo_ready = sem("diff_ready"), sem("diff_hi_ready"), sem("diff_lo_ready")
        pool_done, pool_hi_ready = sem("pool_done"), sem("pool_hi_ready")
        misc_turned = sem("misc_turned")
        misc_taken = [sem("misc_taken_by_scalar"), sem("misc_taken_by_vector")]
        mem_gained = sem("mem_gained")
        gained_ready, act_hi_ready, squared = sem("gained_ready"), sem("act_hi_ready"), sem("squared")
        sum_ready, mean_done, root_done, rms_ready = sem("sum_ready"), sem("mean_done"), sem("root_done"), sem("rms_ready")
        mem_squared = sem("mem_squared")
        mem_stat_act, mem_stat_dve = sem("mem_stat_act"), sem("mem_stat_dve")
        kv_out, kv_free, kv_hi = sem("kv_out"), sem("kv_free"), sem("kv_hi")
        kv_lo, cached_lo = sem("kv_lo"), sem("cached_lo")
        kv_stored, ck_landed, cv_landed = sem("kv_stored"), sem("ck_landed"), sem("cv_landed")
        mk_turned, mk_hi_done, mk_ready = sem("mk_turned"), sem("mk_hi_done"), sem("mk_ready")
        mq_hi = sem("mq_hi")
        ms_done, ms_max, ms_exp, ms_prob = sem("ms_done"), sem("ms_max"), sem("ms_exp"), sem("ms_prob")
        mt_done, mt_hi, mt_ready = sem("mt_done"), sem("mt_hi"), sem("mt_ready")
        mo_done, mo_hi, mo_ready = sem("mo_done"), sem("mo_hi"), sem("mo_ready")
        conv_second, mq_ready = sem("conv_second"), sem("mq_ready")
        gate_ready, conv_first, conv_ready, silu_ready = sem("gate_ready"), sem("conv_first"), sem("conv_ready"), sem("silu_ready")
        hidden_ready, hidden_hi = sem("hidden_ready"), sem("hidden_hi")
        hidden_free = sem("hidden_free")
        conv_turned, conv_tok_ready = sem("conv_turned"), sem("conv_tok_ready")
        y_turned, y_squared, y_root, y_ready = sem("y_turned"), sem("y_squared"), sem("y_root"), sem("y_ready")
        g_final_landed = sem("g_final_landed")
        stored, y_stored = sem("stored"), sem("y_stored")
        act_link, dve_link, pool_link = sem("act_link"), sem("dve_link"), sem("pool_link")
        block = ctx.enter_context(nc.Block())

        def halves(acc):
            return acc[:, :, 0:H]

        def by_half(x):
            return x.rearrange("p (h t) -> p h t", h=2)

        def three(mm, out, w, x, first, last):
            mm(out, w[0], x[0], start=first, stop=False)
            mm(out, w[0], x[1], start=False, stop=False)
            return mm(out, w[1], x[0], start=False, stop=last)

        def project(slot, x_hi, x_lo, acc, feature_tiles, total, ready=None):
            for k in feature_tiles:
                if ready is not None and k == total - 1:
                    nc.tensor.wait_ge(*ready)
                c = slice(k * P, k * P + P)
                for w, x in ((w_hi, x_hi), (w_hi, x_lo), (w_lo, x_hi)):
                    for h in range(2):
                        mm = nc.tensor.matmul(acc[:, h, 0:H], w[slot][:, c], x[:, k, h * H:h * H + H],
                                              start=(k == 0 and w is w_hi and x is x_hi),
                                              stop=(k == total - 1 and w is w_lo))
            if feature_tiles[-1] == total - 1:
                mm.then_inc(weight_used, 1)

        def round_weights(eng, n, slot):
            eng.wait_ge(weight_landed[slot], (n // 2) * 16 + 16 if isinstance(n, int) else n * 8 + (16 - 8 * slot))
            if not isinstance(n, int) or n >= 2:
                eng.wait_ge(weight_used, n - 1)
            nc.scalar.activation(w_hi[slot][:], w_raw[slot][:], ACT.Copy).then_inc(weight_hi_ready, 1)

        def rest_of_weights(eng, n, slot):
            eng.wait_ge(weight_hi_ready, n + 1)
            nc.vector.tensor_tensor(w_lo[slot][:], w_raw[slot][:], w_hi[slot][:].bitcast(F32),
                                    ALU.subtract).then_inc(weight_lo_ready, 1)

        def minus(out, x, hi):
            return nc.vector.tensor_tensor(out, x, hi, ALU.subtract)

        def scaled_minus(out, x, scale, hi):
            return nc.vector.scalar_tensor_tensor(out, x, scale, hi, ALU.mult, ALU.subtract)

        def f32(x):
            return x.bitcast(F32)

        def entry(g):
            j, e = divmod(g, ENTRIES)
            return j, e, e // NT, e % NT

        def keys_of(e):
            return (e % NT + 1) * P if e < 2 * NT else (512 if e < 2 * NT + 2 else TS)

        def probs_done(g):
            j, e = divmod(g, ENTRIES)
            return j * (2 * NT + 1) + min(e, 2 * NT) + 1

        def prompt_slot(g):
            j, e = divmod(g, ENTRIES)
            return (j * 2 * NT + e) % 4

        def prompt_entry_before(g, back):
            j, e = divmod(g, ENTRIES)
            p = j * 2 * NT + e - back
            return None if p < 0 else p // (2 * NT) * ENTRIES + p % (2 * NT)

        def last_prob_turn(t):
            for b in range(t - 2, -1, -2):
                if TURNS[b][0] == "P":
                    return TURNS[b][1]
            return None

        def turns_of(s):
            j, e = divmod(s, ENTRIES)
            found = []
            if j < PAIRS and e in (2, 5):
                found.append(TURN[("K", j, 0 if e == 2 else 1)])
            if s >= LAG and s - LAG < N_ENTRIES:
                found.append(TURN[("P", s - LAG)])
            return found

        OUTPUTS = 3

        def output_of(g):
            j, e = divmod(g, ENTRIES)
            n = e // NT
            return OUTPUTS * j + n, OB[:, n % 2]

        def output_bank_free(n):
            before = {0: n - 1, 1: n - 3, 2: n - 2}[n % OUTPUTS]
            return None if before < 0 else before + 1

        STEPS = N_ENTRIES + LAG + 2

        def weights_after(s):
            j, e = divmod(s, ENTRIES)
            if e == 5 and j < PAIRS:
                return W_QK + 2 * (j + 2)
            return W_QK + 2 * (j + 1) + 1 if e == 1 and j >= 1 else None
        MISCS = ([("k", t) for t in range(NT + 1)] + [("u", 0), ("u", 1), ("f", 0)]
                 + [("x", k) for k in range(KT)] + [("xs", 0)] + [("m", q) for q in range(4)])
        EARLY, MIDDLE, LATE = range(NT + 1), range(NT + 1, NT + 4), range(NT + 4, len(MISCS))
        U_ORDER = [3, 2, 1, 0]
        SAMPLE_MIN = sem("sample_min")

        w_in = a["w_in"][0]
        cols_k = "(k p) c -> p k c"

        def turn_shape(e):
            if e < 2 * NT:
                return P, (e % NT + 1) * P
            return (P, 4 * P) if e < ENTRIES - 1 else (TS, P)

        def output_after(s):
            g = s - LAG - 2
            if g < 0 or g >= N_ENTRIES or g % ENTRIES not in (NT - 1, 2 * NT - 1, ENTRIES - 1):
                return None
            return output_of(g)[0], g

        def output_pieces(n):
            j, m = divmod(n, OUTPUTS)
            bank = OB[:, m % 2]
            k = GROUPS + j
            if m < 2:
                r = slice(m * DH, m * DH + DH)
                return [(lambda x, r=r: x[r, k, 0:TP], bank[r, :])]
            return [(lambda x, h=h: x[h * DH:h * DH + DH, k, TP:T],
                     bank[h * DH:h * DH + DH, h * DH:h * DH + TS]) for h in range(2)]

        def window(engine, g, after):
            src, end = u_all[:, g, :], U_S + TS
            for k in range(g + 1):
                dst, lo = (sum_a, sum_b)[k % 2], 2 ** (k + 1) - 1
                ins = engine.tensor_tensor(dst[:, lo:end], src[:, lo:end], src[:, lo - 2 ** k:end - 2 ** k], ALU.add)
                if k < g:
                    after(ins)
                src = dst[:]
            return ins

        def who(n):
            return n % 2 if MISCS[n][0] != "m" else 0

        def taken(w, n):
            return sum(who(i) == w for i in range(n + 1))

        def take_turns(eng, copy, w, which):
            for n in which:
                kind, m = MISCS[n]
                bank = MISC[n % 4]
                if who(n) != w or kind == "m":
                    continue
                eng.wait_ge(misc_turned, n + 1)
                if kind == "k":
                    r = P if m < NT else TS
                    ins = copy(k_tok[0:r, m, :], bank[0:r, :])
                elif kind == "u":
                    ins = copy(pool_tok[:, m, :], bank[0:NHIST, :])
                elif kind == "f":
                    for t in range(NT + 1):
                        r = P if t < NT else TS
                        ins = copy(gate_tok[0:r, t, :], bank[0:r, t * HEADS:t * HEADS + HEADS])
                elif kind == "x":
                    ins = copy(x_t[:, m, 0:TP], bank)
                else:
                    ins = copy(x_t[:, :, TP:T], bank.rearrange("p (k t) -> p k t", k=KT))
                ins.then_inc(misc_taken[w], 1)

        def memory_scores(s):
            return (ACC[1], SC)[s % 2]

        def memory_bank(m):
            if m < MH:
                return ACC[0][:]
            return ACC[0][:, 0].rearrange("p (k t) -> p k t", k=KT)

        def memory_output(x, m):
            return x[:, 2 * m:2 * m + 2, 0:TP] if m < MH else x[:, :, TP:T]

        def final_bank(t):
            return ps[(t + 1) % 4]

        @block.sync
        def _(sp):
            sp.dma_start(rows_in[0:KT, 0, :], a["g_mix"][0].rearrange("(k p) -> k p", p=P)).then_inc(g_mix_landed, 16)
            for t in (NT, 0, 1, 2, 3):
                x = a["x_prompt"][0, t * P:t * P + P, :] if t < NT else a["x_sample"][0]
                sp.dma_start(x_tok[0:x.shape[0], t, :], x).then_inc(x_landed[t], 16)
            sp.dma_start(rows_in[0:3 * NF, 1, :], a["conv_w"][0].rearrange("j (f p) -> (j f) p", p=P)).then_inc(more_rows_landed, 16)
            sp.dma_start(rows_in[3 * NF:4 * NF, 1, :], a["conv_b"][0].rearrange("(f p) -> f p", p=P)).then_inc(more_rows_landed, 16)
            sp.dma_start(rows_in[0:2 * NF, 2, :], a["state_ffn_conv"][0, 0].rearrange("s (f p) -> (s f) p", p=P)).then_inc(more_rows_landed, 16)
            sp.dma_start(hist_tok[0:NHIST, :], a["state_pool"][0, 0]).then_inc(more_rows_landed, 16)

            def load(n, slot, source, shape=None):
                if not isinstance(n, int) or n >= 2:
                    sp.wait_ge(weight_lo_ready, n - 1)
                dst = w_raw[slot][:]
                if shape is not None:
                    dst = dst[:, 0:shape[0] * shape[1]].rearrange("p (k c) -> p k c", k=shape[0])
                sp.dma_start(dst, source).then_inc(weight_landed[slot], 16)

            v_cols = slice(DPOOL + 2 * DFOX, DPOOL + 3 * DFOX)
            for n in range(4):
                load(W_V + n, n % 2, w_in[2 * n * P:2 * n * P + 2 * P, v_cols].rearrange(cols_k, p=P), (2, DFOX))
            for j in range(PAIRS):
                for c in range(2):
                    at_col = DPOOL + c * DFOX + j * P
                    load(W_QK + 2 * j + c, c, w_in[:, at_col:at_col + P].rearrange(cols_k, p=P), (KT, P))
            for n, g in enumerate(U_ORDER):
                load(W_U + n, n % 2, w_in[:, g * P:g * P + P].rearrange(cols_k, p=P), (KT, P))
            for c in range(2):
                load(W_O + c, c, a["w_o"][0][:, c * P:c * P + P].rearrange(cols_k, p=P), (KT, P))
            sp.wait_ge(turn_done, len(TURNS))
            sp.wait_ge(scores_done, N_ENTRIES)
            sp.wait_ge(vc_ready, PAIRS)
            sp.wait_ge(wp_landed, 16)
            for t in range(NT):
                sp.dma_start(x_again[:, t, :], a["x_prompt"][0, t * P:t * P + P, :]).then_inc(misc_landed, 16)
            sp.dma_start(x_again[0:TS, NT, :], a["x_sample"][0]).then_inc(misc_landed, 16)

            def by_columns(n0, w, k=KT, off=(0, P), step=2 * P, rounds=KT // 2):
                source = w.rearrange(cols_k, p=P)
                with sp.Fori(0, rounds) as i:
                    for c in range(2):
                        load(i * 2 + (n0 + c), c, source[:, :, bass.ds(i * step + off[c], P)], (k, P))

            def by_rows(n0, w, r0, rounds):
                with sp.Fori(0, rounds) as i:
                    for c in range(2):
                        load(i * 2 + (n0 + c), c, w[bass.ds(i * (2 * P) + (r0 + c) * P, P), :])

            by_columns(W_O + 2, a["w_o"][0], off=(2 * P, 3 * P), rounds=KT // 2 - 1)
            by_rows(W_MK, a["w_mk"][0], 0, KT // 2)
            by_columns(W_MQ, a["w_mq"][0])
            by_rows(W_MV, a["w_mv"][0], 0, KT // 2)
            by_columns(W_MO, a["w_mo"][0])
            for k, (f0, nf) in enumerate(CHUNKS):
                by_columns(W_UP[k], a["w_up"][0], off=(f0 * P, DFF + f0 * P), step=P, rounds=nf)
                by_columns(W_DOWN[k], a["w_down"][0, f0 * P:(f0 + nf) * P, :], k=nf)
            for t in range(NT + 1):
                sp.wait_ge(y_ready, t + 1)
                y = o["y_prompt"][0, t * P:t * P + P, :] if t < NT else o["y_sample"][0]
                sp.dma_start(y, y_tok[0:y.shape[0], t, :]).then_inc(y_stored, 16)
            sp.wait_ge(y_stored, 16 * (NT + 1))
            N_STORED = 2 + 2 + 2 + 2 + 2 + 2
            sp.wait_ge(stored, 16 * N_STORED)

        @block.gpsimd
        def _(pool):
            link = Tally(pool_link)

            def after(ins):
                link.inc(ins)
                pool.wait_ge(pool_link, link.now)

            def small(dst, src):
                pool.dma_start(dst, src).then_inc(small_landed, 16)

            nc.gpsimd.memset(eps[:], EPS).then_inc(early_ready, 1)
            nc.gpsimd.memset(stat[:], 1.0).then_inc(early_ready, 1)
            after(nc.gpsimd.memset(ident[:], 0.0))
            nc.gpsimd.affine_select(out=ident[:], in_=ident[:], compare_op=ALU.not_equal, fill=1.0, base=0,
                                    pattern=[[-1, P]], channel_multiplier=1).then_inc(early_ready, 1)
            n = KT
            for name in ("g_xq", "g_mkv", "g_ffn"):
                pool.dma_start(rows_in[n:n + KT, 0, :], a[name][0].rearrange("(k p) -> k p", p=P)).then_inc(rows_landed, 16)
                n += KT
            pool.dma_start(rows_in[n:NG, 0, :], a["pool_scale"][0].rearrange("(k p) -> k p", p=P)).then_inc(rows_landed, 16)
            nc.gpsimd.memset(one[:], 1.0).then_inc(consts_ready, 1)
            nc.gpsimd.memset(mean_w[:], 1.0 / D).then_inc(consts_ready, 1)
            for x in flat_a + flat_b:
                nc.gpsimd.memset(f32(x[:, KT * T:]), 0.0).then_inc(consts_ready, 1)
            for x in (wf_hi, wf_lo, qs_hi, qs_lo):
                nc.gpsimd.memset(f32(x[:]), 0.0).then_inc(consts_ready, 1)
            small(wf_raw[:], w_in[:, D_IN - HEADS:D_IN].rearrange(cols_k, p=P))
            small(b_f[:], a["b_f"][0].rearrange("(h x) -> h x", x=1))
            small(cl_tok[:], a["cache_fox_logf"][0, 0].rearrange("(c p) h -> p c h", p=P))
            after(nc.gpsimd.memset(causal[:], 0.0))
            nc.gpsimd.affine_select(out=causal[:], in_=causal[:], compare_op=ALU.is_ge, fill=MASKED, base=0,
                                    pattern=[[-1, P]], channel_multiplier=1).then_inc(masks_ready, 1)
            for t in range(16):
                nc.gpsimd.memset(early_count[:, t:t + 1], 1.0 / (t + 1))
            pool.wait_ge(cols_turned, 2)
            nc.gpsimd.memset(u_all[:, :, 0:NHIST], 0.0).then_inc(masks_ready, 1)
            pool.wait_ge(v_copied, NT + 1)
            pool.dma_start(o["fox_v_prompt"][0, 0].rearrange("(t p) h d -> p t (h d)", p=P), v_out[:, 0:NT, :]).then_inc(stored, 16)
            pool.dma_start(o["fox_v_sample"][0, 0].rearrange("t h d -> t (h d)"), v_out[0:TS, NT, :]).then_inc(stored, 16)
            pool.wait_ge(cum_ready, 2)
            pool.dma_start(decay_p_dram, cum_p[:]).then_inc(cum_stored, 16)
            pool.dma_start(decay_s_dram, cum_s[:]).then_inc(cum_stored, 16)
            pool.wait_ge(cum_stored, 32)
            pool.wait_ge(stored, 32)

            def load_decay_prompt(j):
                if j >= 2:
                    pool.wait_ge(scores_taken, ENTRIES * (j - 2) + 2 * NT)
                for h in range(2):
                    row = decay_p_dram[2 * j + h:2 * j + h + 1, :]
                    pool.dma_start(decay_p[:, j % 2, h, :], row.partition_broadcast(P)).then_inc(decay_landed[j % 2], 16)

            def load_sample(j):
                if j >= 1:
                    pool.wait_ge(scores_taken, ENTRIES * j)
                for h in range(2):
                    row = decay_s_dram[2 * j + h:2 * j + h + 1, :]
                    pool.dma_start(decay_s[h * DH:h * DH + DH, :], row.partition_broadcast(DH)).then_inc(decay_s_landed, 16)

            def load_cache(j):
                heads = slice(2 * j, 2 * j + 2)
                if j >= 1:
                    pool.wait_ge(turn_done, TURN[("K", j - 1, 1)] + 1)
                pool.dma_start(kc_raw[:], a["cache_fox_k"][0, 0, :, heads, :].rearrange("(c p) h d -> p c (h d)", p=P)).then_inc(cache_k_landed, 16)
                if j >= 1:
                    pool.wait_ge(vc_ready, j)
                pool.dma_start(vc_raw[:], a["cache_fox_v"][0, 0, :, heads, :].rearrange("(c p) h d -> p c (h d)", p=P)).then_inc(cache_v_landed, 16)

            load_decay_prompt(0)
            load_cache(0)
            load_sample(0)
            load_decay_prompt(1)
            for j in range(1, PAIRS):
                load_cache(j)
                load_sample(j)
                if j + 1 < PAIRS:
                    load_decay_prompt(j + 1)
            pool.wait_ge(scores_taken, N_ENTRIES - 3)
            pool.wait_ge(acc_free, A_U + 1)
            window(nc.gpsimd, U_ORDER[0], after).then_inc(window_ready, 1)
            pool.wait_ge(pv_done, N_ENTRIES)
            pool.dma_start(wp_raw[:], a["w_pool"][0].rearrange("g c d -> c g d")).then_inc(wp_landed, 16)
            pool.wait_ge(weight_used, W_O)
            pool.dma_start(mem_tok[:], a["mem_prompt"][0].rearrange("(t p) d -> p t d", p=P)).then_inc(mem_landed, 16)
            for w in range(2):
                pool.wait_ge(misc_taken[w], taken(w, NT))
            pool.dma_start(o["fox_k_prompt"][0, 0].rearrange("(t p) h d -> p t (h d)", p=P), k_tok[:, 0:NT, :]).then_inc(stored, 16)
            pool.dma_start(o["fox_k_sample"][0, 0].rearrange("t h d -> t (h d)"), k_tok[0:TS, NT, :]).then_inc(stored, 16)
            for w in range(2):
                pool.wait_ge(misc_taken[w], taken(w, NT + 3))
            pool.dma_start(o["pool_state_prompt"][0, 0], pool_tok[:, 0, :]).then_inc(stored, 16)
            pool.dma_start(o["pool_state_sample"][0, 0], pool_tok[:, 1, :]).then_inc(stored, 16)
            pool.dma_start(o["fox_logf_prompt"][0, 0].rearrange("(t p) h -> p t h", p=P), gate_tok[:, 0:NT, :]).then_inc(stored, 16)
            pool.dma_start(o["fox_logf_sample"][0, 0], gate_tok[0:TS, NT, :]).then_inc(stored, 16)
            pool.wait_ge(kv_out, 2)
            pool.dma_start(o["mem_k_prompt"][0, 0].rearrange("(t p) h d -> p t (h d)", p=P), kv_tok[:]).then_inc(stored, 16)
            pool.wait_ge(stored, 16 * 9)
            pool.wait_ge(mk_turned, 4)
            pool.dma_start(kv_tok[:], a["cache_mem_k"][0, 0].rearrange("(t p) h d -> p t (h d)", p=P)).then_inc(ck_landed, 16)
            pool.wait_ge(kv_out, 4)
            pool.dma_start(o["mem_v_prompt"][0, 0].rearrange("(t p) h d -> p t (h d)", p=P), kv_tok[:]).then_inc(stored, 16)
            pool.wait_ge(stored, 16 * 10)
            pool.wait_ge(kv_lo, 1)
            pool.dma_start(kv_tok[:], a["cache_mem_v"][0, 0].rearrange("(t p) h d -> p t (h d)", p=P)).then_inc(cv_landed, 16)
            for t in range(MT):
                pool.wait_ge(kv_hi, 2 + t)
                nc.gpsimd.tensor_tensor(mv_lo[:, 1, t, :], kv_tok[:, t, :], f32(mv_hi[:, 1, t, :]),
                                        ALU.subtract).then_inc(cached_lo, 1)
            pool.wait_ge(acc_free, A_UP[0])
            pool.dma_start(g_final[:], a["g_final"].rearrange("(x d) -> x d", x=1).partition_broadcast(P)).then_inc(g_final_landed, 16)
            pool.wait_ge(conv_tok_ready, 1)
            pool.dma_start(o["conv_state_prompt"][0, 0].rearrange("s (f p) -> (s f) p", p=P), conv_tok[0:2 * NF, :]).then_inc(stored, 16)
            pool.dma_start(o["conv_state_sample"][0, 0].rearrange("s (f p) -> (s f) p", p=P), conv_tok[2 * NF:4 * NF, :]).then_inc(stored, 16)

        @block.scalar
        def _(act):
            link = Tally(act_link)

            def after(ins):
                link.inc(ins)
                act.wait_ge(act_link, link.now)

            def copy(out, x, scale=1.0):
                return nc.scalar.activation(out, x, ACT.Copy, scale=scale)

            act.wait_ge(early_ready, 2)
            nc.scalar.activation(stat[:, 60:61], stat[:, 61:62], ACT.Sqrt)
            for n, t in enumerate((NT, 0, 1, 2, 3)):
                r = P if t < NT else TS
                act.wait_ge(x_landed[t], 16)
                nc.scalar.activation(square[0:r, :], x_tok[0:r, t, :], ACT.Square,
                                     accum_out=stat[0:r, t:t + 1]).then_inc(x_squared, 1)
                act.wait_ge(x_squared, n + 1)
                nc.scalar.activation(stat[0:r, 8 + t:9 + t], stat[0:r, t:t + 1], ACT.Sqrt, bias=eps[0:r],
                                     scale=1.0 / D).then_inc(x_rms, 1)
            act.wait_ge(hs_gained, 1)
            copy(a_hi[:, :, TP:T], x_gained_s[:]).then_inc(hs_hi_ready, 1)
            round_weights(act, 0, 0)
            for k in range(KT):
                if k == 2:
                    round_weights(act, 1, 1)
                act.wait_ge(h_turned, k + 1)
                copy(a_hi[:, k, 0:TP], (SC[:, 1], OB[:, 0])[k % 2], g_mix[:, k:k + 1]).then_inc(h_hi_ready, 1)
                if k in (3, 5):
                    round_weights(act, (k + 1) // 2, (k + 1) // 2 % 2)
            act.wait_ge(consts_ready, 10)
            act.wait_ge(small_landed, 48)
            copy(wf_hi[:, :, 0:HEADS], wf_raw[:]).then_inc(wf_hi_ready, 1)
            round_weights(act, 4, 0)
            round_weights(act, 5, 1)
            act.wait_ge(weight_used, 4)
            for t in (NT, 0, 1, 2, 3):
                r = P if t < NT else TS
                bank = (ACC[t // 2][:, t % 2] if t < NT else SC[0:TS, 0])
                copy(v_hi[:, t, :] if t < NT else own_hi[:], bank)
                copy(v_out[0:r, t, :], bank).then_inc(v_copied, 1)
            act.wait_ge(gate_dve, 1)
            after(nc.scalar.activation(z_abs[:], z[:], ACT.Abs))
            after(nc.scalar.activation(z_abs[:], z_abs[:], ACT.Exp, scale=-1.0))
            nc.scalar.activation(z_abs[:], z_abs[:], ACT.Ln, bias=one[0:HEADS]).then_inc(gate_act, 1)

            def finish_q(j):
                n, b, acc = W_QK + 2 * j, j % 2, ACC[0]
                act.wait_ge(weight_used, n + 1)
                if j >= 2:
                    act.wait_ge(scores_done, ENTRIES * (j - 1))
                copy(q_hi[:, b, 0:H], acc[:, 0, 0:H], QSCALE)
                copy(q_hi[:, b, H:TP], acc[:, 1, 0:TP - H], QSCALE)
                for h in range(2):
                    r = slice(h * DH, h * DH + DH)
                    ins = copy(qs_hi[r, b, h * DH:h * DH + DH], acc[r, 1, TP - H:H], QSCALE)
                ins.then_inc(qk_hi_ready, 1)

            def finish_k(j):
                n, b, acc = W_QK + 2 * j + 1, j % 2, ACC[j == 0]
                act.wait_ge(weight_used, n + 1)
                copy(by_half(k_hi[:, b, :]), halves(acc))
                copy(by_half(k_new[:, j, :]), halves(acc)).then_inc(qk_hi_ready, 1)

            round_weights(act, 6, 0)
            finish_q(0)
            finish_k(0)
            round_weights(act, 7, 1)

            for s in range(STEPS):
                j, e = divmod(s, ENTRIES)
                if e in (5, 10) and j < PAIRS:
                    if j + 1 < PAIRS:
                        (finish_q, finish_k)[e // 10](j + 1)
                if e == 6 and j < PAIRS:
                    act.wait_ge(cache_v_landed, 16 * (j + 1))
                    if j >= 1:
                        act.wait_ge(pv_done, ENTRIES * j)
                    copy(vc_hi[:], vc_raw[:]).then_inc(vc_hi_ready, 1)
                def exponentials():
                    if s < N_ENTRIES:
                        if e < 2 * NT:
                            act.wait_ge(scores_taken, s + 1)
                            p = prob_p[:, prompt_slot(s), 0:keys_of(e)]
                            nc.scalar.activation(p, p, ACT.Exp, bias=fox_stat[:, s, 0:1], scale=-1.0,
                                                 accum_out=fox_stat[:, s, 1:2]).then_inc(exp_done, 1)
                        elif e == ENTRIES - 1:
                            act.wait_ge(SAMPLE_MIN, j + 1)
                            nc.scalar.activation(prob_s[:], prob_s[:], ACT.Exp, bias=fox_stat[:, s, 3:4],
                                                 scale=-1.0, accum_out=fox_stat[:, s, 1:2]).then_inc(exp_done, 1)

                if e < ENTRIES - 1:
                    exponentials()
                for t in turns_of(s):
                    what = TURNS[t]
                    act.wait_ge(turn_done, t + 1)
                    if what[0] == "K":
                        if what[1] >= 1:
                            act.wait_ge(scores_done, ENTRIES * what[1])
                        copy(kc_hi[:, what[2] * 512:what[2] * 512 + 512], TB[t % 2]).then_inc(turn_hi_ready, 1)
                    else:
                        e_t = what[1] % ENTRIES
                        rows, width = turn_shape(e_t)
                        if last_prob_turn(t) is not None:
                            act.wait_ge(pv_done, last_prob_turn(t) + 1)
                        copy(pt_hi[0:rows, t % 2, 0:width], TB[t % 2][0:rows, 0:width]).then_inc(turn_hi_ready, 1)
                if e == ENTRIES - 1:
                    exponentials()
                out = output_after(s)
                if out is not None:
                    n, g = out
                    act.wait_ge(pv_done, g + 1)
                    for d, b in output_pieces(n):
                        ins = copy(d(b_hi), b)
                    ins.then_inc(o_hi_ready, 1)
                if weights_after(s) is not None:
                    round_weights(act, weights_after(s), weights_after(s) % 2)
            def pool_operand(n):
                act.wait_ge(diff_ready, n + 1)
                if n >= 2:
                    act.wait_ge(pool_done, n - 1)
                copy(diff_hi[:, n % 2, :], diff[:, n % 2, :]).then_inc(diff_hi_ready, 1)

            def pool_result(n):
                g = U_ORDER[n]
                act.wait_ge(pool_done, n + 1)
                copy(by_half(b_hi[:, g, :]), halves(ACC[n % 2]), pool_scale[:, g:g + 1]).then_inc(pool_hi_ready, 1)

            act.wait_ge(pv_done, N_ENTRIES)
            pool_operand(0)
            pool_operand(1)
            act.wait_ge(wp_landed, 16)
            copy(wp_hi[:], wp_raw[:]).then_inc(wp_hi_ready, 1)
            round_weights(act, W_O, 0)
            pool_operand(2)
            pool_result(0)
            pool_operand(3)
            pool_result(1)
            take_turns(act, copy, 0, EARLY)
            pool_result(2)
            pool_result(3)
            round_weights(act, W_O + 1, 1)
            take_turns(act, copy, 0, MIDDLE)
            act.wait_ge(mem_landed, 16)
            for t in range(MT):
                ins = nc.scalar.activation(mem_squares[:, t, :], mem_tok[:, t, :], ACT.Square,
                                           accum_out=stat[:, 16 + t:17 + t])
            ins.then_inc(mem_squared, 1)
            take_turns(act, copy, 0, LATE)
            for q in range(4):
                n = len(MISCS) - 4 + q
                act.wait_ge(misc_turned, n + 1)
                for c in range(2):
                    k = 2 * q + c
                    ins = copy(mem_hi[:, k, :], MISC[n % 4][:, c * MEM:c * MEM + MEM], g_mkv[:, k:k + 1])
                ins.then_inc(misc_taken[0], 1)

            def residual_steps(w0, first, sums):
                with act.Fori(0, KT // 2) as i:
                    for c in range(2):
                        k = i * 2 + c
                        round_weights(act, k + (w0 + 2), c)
                        act.wait_ge(gained_ready, k + (first + 1))
                        copy((a_hi if first == 0 else b_hi)[:, bass.ds(k, 1), :].rearrange("p k t -> p (k t)"),
                             gained[:]).then_inc(act_hi_ready, 1)
                        act.wait_ge(sum_ready, k + sums)
                        nc.scalar.activation(squares[:], x_t[:, bass.ds(k, 1), :].rearrange("p k t -> p (k t)"),
                                             ACT.Square).then_inc(squared, 1)

            def root(n, bank):
                act.wait_ge(mean_done, n)
                nc.scalar.activation(by_half(inv_rms[:]), bank[:, :, 0:H], ACT.Sqrt, bias=eps[:]).then_inc(root_done, 1)

            residual_steps(W_O, 0, 1)
            with act.Fori(0, KT // 2) as i:
                for c in range(2):
                    round_weights(act, i * 2 + (W_MK + 2 + c), c)
            act.wait_ge(mem_squared, 1)
            nc.scalar.activation(stat[:, 18:20], stat[:, 16:18], ACT.Sqrt, bias=eps[:],
                                 scale=1.0 / D).then_inc(mem_stat_act, 1)
            root(1, ACC[1])
            act.wait_ge(mem_stat_dve, 1)
            act.wait_ge(stored, 16 * 8)
            for t in range(MT):
                copy(kv_tok[:, t, :].rearrange("p (b c) -> p b c", b=2), (SC, OB)[t][:], stat[:, 20 + t:21 + t]).then_inc(kv_out, 1)
            with act.Fori(0, KT // 2) as i:
                for c in range(2):
                    k = i * 2 + c
                    round_weights(act, k + (W_MQ + 2), c)
                    act.wait_ge(acc_free, k + (A_MQ + 1))
                    copy(b_hi[:, bass.ds(k, 1), :].rearrange("p k t -> p (k t)"), gained[:], MSCALE).then_inc(mq_hi, 1)

            def memory_keys(s):
                for q in range(4):
                    act.wait_ge(mk_turned, 4 * s + q + 1)
                    copy(mk_hi[:, s, 2 * q:2 * q + 2, :], ACC[q // 2][:, q % 2].rearrange("p (k m) -> p k m", k=2)).then_inc(mk_hi_done, 1)

            def exponentials_of(s):
                r = P if s < MH else TS
                act.wait_ge(ms_max, s + 1)
                for q in range(4):
                    ins = nc.scalar.activation(mp[0:r, s % 2, q, :], memory_scores(s)[0:r, q // 2, q % 2 * MEM:q % 2 * MEM + MEM], ACT.Exp,
                                               bias=stat[0:r, 28 + q:29 + q], accum_out=stat[0:r, 32 + q:33 + q])
                ins.then_inc(ms_exp, 1)

            for k in range(KT):
                round_weights(act, W_MV + 2 + k, k % 2)
                if k in (0, 3):
                    memory_keys(k // 3)
                if k == 5:
                    exponentials_of(0)
            act.wait_ge(weight_used, W_MV + KT)
            for t in range(MT):
                bank = (SC, OB)[t]
                copy(kv_tok[:, t, :].rearrange("p (b c) -> p b c", b=2), bank[:], stat[:, 20 + t:21 + t]).then_inc(kv_out, 1)
            act.wait_ge(kv_out, 4)
            copy(mv_hi[:, 0], kv_tok[:]).then_inc(kv_hi, 1)

            for s in range(MH + 1 + 2):
                if 1 <= s <= MH:
                    exponentials_of(s)
                if s >= 2:
                    m = s - 2
                    act.wait_ge(mo_done, m + 1)
                    copy(memory_output(a_hi, m), memory_bank(m)).then_inc(mo_hi, 1)
                if 1 <= s <= MH + 1:
                    m = s - 1
                    w = TP if m < MH else MH * TS
                    act.wait_ge(mt_done, m + 1)
                    copy(mpt_hi[:, :, 0:w], OB[:, :, 0:w]).then_inc(mt_hi, 1)
                if s in (3, 4):
                    t = s - 3
                    act.wait_ge(cv_landed, 16)
                    copy(mv_hi[:, 1, t, :], kv_tok[:, t, :]).then_inc(kv_hi, 1)

            residual_steps(W_MO, KT, KT + 2)
            root(2, SC)
            nc.scalar.activation(stat[:, 60:61], stat[:, 61:62], ACT.Silu)
            for k, (f0, nf) in enumerate(CHUNKS):
                with act.Fori(0, nf) as i:
                    round_weights(act, i * 2 + (W_UP[k] + 2), 0)
                    act.wait_ge(gate_ready, i + (f0 + 1))
                    nc.scalar.activation(conv_a[:, 2:TE], gate[:, 2:TE], ACT.Identity, bias=par[:, 3:4],
                                         scale=par[:, 2:3]).then_inc(conv_first, 1)
                    act.wait_ge(conv_ready, i + (f0 + 1))
                    act.wait_ge(hidden_free, i + (f0 + 1))
                    nc.scalar.activation(silu[:, 0:TE - 2], conv_a[:, 2:TE], ACT.Silu).then_inc(silu_ready, 1)
                    act.wait_ge(hidden_ready, i + (f0 + 1))
                    copy(a_hi[:, bass.ds(i, 1), :].rearrange("p k t -> p (k t)"), hidden[:]).then_inc(hidden_hi, 1)
                    round_weights(act, i * 2 + (W_UP[k] + 3), 1)
                with act.Fori(0, KT // 2 - (k == 2)) as i:
                    for c in range(2):
                        round_weights(act, i * 2 + (W_DOWN[k] + 2 + c), c)
            act.wait_ge(conv_turned, 1)
            copy(conv_tok[:], MISC[0][0:4 * NF, 0:P]).then_inc(conv_tok_ready, 1)
            for t in range(NT + 1):
                r = P if t < NT else TS
                act.wait_ge(y_turned, t + 1)
                nc.scalar.activation(y_junk[0:r, :].rearrange("p (b c) -> p b c", b=2), final_bank(t)[0:r], ACT.Square,
                                     accum_out=stat[0:r, 40 + t:41 + t]).then_inc(y_squared, 1)
                act.wait_ge(y_squared, t + 1)
                nc.scalar.activation(stat[0:r, 48 + t:49 + t], stat[0:r, 40 + t:41 + t], ACT.Sqrt, bias=eps[0:r],
                                     scale=1.0 / D).then_inc(y_root, 1)

        @block.vector
        def _(dve):
            link = Tally(dve_link)
            add, mult, sub = ALU.add, ALU.mult, ALU.subtract

            def after(ins):
                link.inc(ins)
                dve.wait_ge(dve_link, link.now)

            bank = OB[:, 1]
            for n, t in enumerate((NT, 0, 1, 2, 3)):
                r = P if t < NT else TS
                dve.wait_ge(x_rms, n + 1)
                after(nc.vector.reciprocal(stat[0:r, 48 + t:49 + t], stat[0:r, 8 + t:9 + t]))
                nc.vector.tensor_scalar(xr_tok[0:r, t, :], x_tok[0:r, t, :], stat[0:r, 48 + t:49 + t], None,
                                        mult).then_inc(xr_ready, 1)
                if t == 1:
                    dve.wait_ge(cols_turned, 1)
                    nc.vector.tensor_copy(g_mix, bank[:, 0:KT]).then_inc(cols_ready, 1)
                if t == 2:
                    dve.wait_ge(hs_turned, 1)
                    dve.wait_ge(cols_ready, 1)
                    nc.vector.tensor_tensor(x_gained_s[:], SC[:, 0].rearrange("p (k t) -> p k t", k=KT),
                                            g_mix.unsqueeze(2).to_broadcast([P, KT, TS]), mult).then_inc(hs_gained, 1)
            dve.wait_ge(hs_hi_ready, 1)
            minus(a_lo[:, :, TP:T], x_gained_s[:], f32(a_hi[:, :, TP:T])).then_inc(hs_lo_ready, 1)
            rest_of_weights(dve, 0, 0)
            for k in range(KT):
                if k == 2:
                    rest_of_weights(dve, 1, 1)
                dve.wait_ge(h_hi_ready, k + 1)
                scaled_minus(a_lo[:, k, 0:TP], (SC[:, 1], OB[:, 0])[k % 2], g_mix[:, k:k + 1],
                             f32(a_hi[:, k, 0:TP])).then_inc(h_lo_ready, 1)
                if k in (3, 5):
                    rest_of_weights(dve, (k + 1) // 2, (k + 1) // 2 % 2)
            dve.wait_ge(wf_hi_ready, 1)
            minus(wf_lo[:, :, 0:HEADS], wf_raw[:], f32(wf_hi[:, :, 0:HEADS])).then_inc(wf_ready, 1)
            dve.wait_ge(consts_ready, 10)
            nc.vector.tensor_copy(ident_r[:], ident[:]).then_inc(masks_split, 1)
            dve.wait_ge(masks_ready, 1)
            nc.vector.tensor_copy(causal_r[:], causal[:]).then_inc(masks_split, 1)
            for h in range(2):
                r = slice(h * DH, h * DH + DH)
                nc.vector.tensor_copy(causal_s[r, :], causal[r, r]).then_inc(masks_split, 1)
            dve.wait_ge(cols_turned, 2)
            nc.vector.tensor_copy(gains[:, KT:NG], bank[:, KT:NG])
            nc.vector.tensor_copy(conv_par[:].rearrange("p j f -> p (j f)"), bank[:, 64:64 + 4 * NF]).then_inc(cols_ready, 1)
            nc.vector.tensor_copy(conv_hist[:].rearrange("p s f -> p (s f)"), bank[:, 192:192 + 2 * NF]).then_inc(cols_ready, 1)
            dve.wait_ge(masks_ready, 2)
            nc.vector.tensor_copy(u_all[:, :, NHIST + TP:U_S],
                                  bank[:, 256:256 + 16 * GROUPS].rearrange("p (g t) -> p g t", t=16)[:, :, 0:NHIST]).then_inc(cols_ready, 1)
            rest_of_weights(dve, 4, 0)
            rest_of_weights(dve, 5, 1)
            for n, t in enumerate((NT, 0, 1, 2, 3)):
                bank = (ACC[t // 2][:, t % 2] if t < NT else SC[0:TS, 0])
                lo, hi = (v_lo[:, t, :], v_hi[:, t, :]) if t < NT else (own_lo[:], own_hi[:])
                dve.wait_ge(v_copied, n + 1)
                minus(lo, bank, f32(hi)).then_inc(v_free, 1)
            dve.wait_ge(gate_done, 1)
            nc.vector.tensor_scalar(by_half(z[:]), OB[0:HEADS, :, 0:H], b_f[:], None, add).then_inc(gate_dve, 1)
            dve.wait_ge(gate_dve, 1)
            after(nc.vector.tensor_scalar(z_min[:], z[:], 0.0, None, ALU.min))
            after(nc.vector.memset(ones_row[:], 1.0))
            dve.wait_ge(gate_act, 1)
            after(minus(logf[:], z_min[:], z_abs[:]))
            dve.wait_ge(gate_done, 2)
            nc.vector.tensor_copy(log_s[:, 0:PAST].rearrange("h (b t) -> h b t", b=2), SC[0:HEADS]).then_inc(gate_dve, 1)
            nc.vector.tensor_copy(log_s[:, PAST:KEYS], logf[:, TP:T]).then_inc(gate_dve, 1)
            dve.wait_ge(gate_dve, 3)
            nc.vector.tensor_tensor_scan(cum_p[:], ones_row[:, 0:TP], logf[:, 0:TP], 0.0, mult, sub).then_inc(cum_ready, 1)
            nc.vector.tensor_tensor_scan(cum_s[:], ones_row[:], log_s[:], 0.0, mult, sub).then_inc(cum_ready, 1)

            def finish_q(j):
                b, acc = j % 2, ACC[0]
                dve.wait_ge(qk_hi_ready, 2 * j + 1)
                scaled_minus(q_lo[:, b, 0:H], acc[:, 0, 0:H], QSCALE, f32(q_hi[:, b, 0:H]))
                scaled_minus(q_lo[:, b, H:TP], acc[:, 1, 0:TP - H], QSCALE, f32(q_hi[:, b, H:TP]))
                for h in range(2):
                    r = slice(h * DH, h * DH + DH)
                    ins = scaled_minus(qs_lo[r, b, r], acc[r, 1, TP - H:H], QSCALE, f32(qs_hi[r, b, r]))
                ins.then_inc(acc_free, 1)

            def finish_k(j):
                b, acc = j % 2, ACC[j == 0]
                dve.wait_ge(qk_hi_ready, 2 * j + 2)
                minus(by_half(k_lo[:, b, :]), halves(acc), by_half(f32(k_hi[:, b, :]))).then_inc(acc_free, 1)

            def finish_u(n, slot):
                g, acc = U_ORDER[n], ACC[slot]
                dve.wait_ge(weight_used, W_U + n + 1)
                nc.vector.tensor_copy(u_all[:, g, NHIST:NHIST + H], acc[:, 0, 0:H])
                nc.vector.tensor_copy(u_all[:, g, NHIST + H:NHIST + TP], acc[:, 1, 0:TP - H])
                nc.vector.tensor_copy(u_all[:, g, U_S:U_S + TS], acc[:, 1, TP - H:H]).then_inc(acc_free, 1)

            rest_of_weights(dve, 6, 0)
            finish_q(0)
            finish_k(0)
            rest_of_weights(dve, 7, 1)

            for s in range(STEPS):
                j, e = divmod(s, ENTRIES)
                if e in (5, 10) and j < PAIRS:
                    if j + 1 < PAIRS:
                        (finish_q, finish_k)[e // 10](j + 1)
                    else:
                        finish_u(e // 10, 0)
                if s < N_ENTRIES:
                    dve.wait_ge(scores_done, s + 1)
                    if e == 0:
                        dve.wait_ge(decay_landed[j % 2], 32 * (j // 2 + 1))
                    if e < 2 * NT:
                        before = prompt_entry_before(s, 4)
                        if before is not None:
                            dve.wait_ge(turn_done, TURN[("P", before)] + 1)
                        w = keys_of(e)
                        nc.vector.tensor_tensor_reduce(
                            prob_p[:, prompt_slot(s), 0:w], SC[:, s % 2, 0:w], decay_p[:, j % 2, e // NT, 0:w],
                            -1.0, 3e38, add, ALU.min, fox_stat[:, s, 0:1]).then_inc(scores_taken, 1)
                    else:
                        c = e - 2 * NT
                        if c == 0:
                            dve.wait_ge(decay_s_landed, 32 * (j + 1))
                            if j >= 1:
                                dve.wait_ge(turn_done, TURN[("P", ENTRIES * j - 1)] + 1)
                        w = keys_of(e)
                        nc.vector.tensor_tensor_reduce(
                            prob_s[:, c * 512:c * 512 + w], SC[:, s % 2, 0:w], decay_s[:, c * 512:c * 512 + w],
                            -1.0, 3e38, add, ALU.min, fox_stat[:, s, 0:1]).then_inc(scores_taken, 1)
                        if c == 2:
                            dve.wait_ge(scores_taken, s + 1)
                            nc.vector.tensor_reduce(fox_stat[:, s, 3:4], fox_stat[:, s - 2:s + 1, 0], X,
                                                    ALU.min).then_inc(SAMPLE_MIN, 1)
                if e == 7 and j < PAIRS:
                    dve.wait_ge(vc_hi_ready, j + 1)
                    minus(vc_lo[:], vc_raw[:], f32(vc_hi[:])).then_inc(vc_ready, 1)
                g = s - 1
                if 0 <= g < N_ENTRIES and (g % ENTRIES < 2 * NT or g % ENTRIES == ENTRIES - 1):
                    dve.wait_ge(exp_done, probs_done(g))
                    after(nc.vector.reciprocal(fox_stat[:, g, 2:3], fox_stat[:, g, 1:2]))
                    p = (prob_p[:, prompt_slot(g), 0:keys_of(g % ENTRIES)] if g % ENTRIES < 2 * NT else prob_s[:])
                    nc.vector.tensor_scalar(p, p, fox_stat[:, g, 2:3], None, mult).then_inc(prob_ready, 1)
                for t in turns_of(s):
                    what = TURNS[t]
                    dve.wait_ge(turn_hi_ready, t + 1)
                    if what[0] == "K":
                        c = slice(what[2] * 512, what[2] * 512 + 512)
                        minus(kc_lo[:, c], TB[t % 2], f32(kc_hi[:, c])).then_inc(turn_ready, 1)
                    else:
                        rows, w = turn_shape(what[1] % ENTRIES)
                        minus(pt_lo[0:rows, t % 2, 0:w], TB[t % 2][0:rows, 0:w],
                              f32(pt_hi[0:rows, t % 2, 0:w])).then_inc(turn_ready, 1)
                out = output_after(s)
                if out is not None:
                    dve.wait_ge(o_hi_ready, out[0] + 1)
                    for d, b in output_pieces(out[0]):
                        ins = minus(d(b_lo), b, f32(d(b_hi)))
                    ins.then_inc(o_free, 1)
                if weights_after(s) is not None:
                    rest_of_weights(dve, weights_after(s), weights_after(s) % 2)

            def mix(n):
                g = U_ORDER[n]
                w = 2 ** (g + 1)
                total, u, d = (sum_a, sum_b)[g % 2], u_all[:, g, :], diff[:, n % 2, :]
                if n == 0:
                    dve.wait_ge(window_ready, 1)
                else:
                    dve.wait_ge(diff_ready, n)
                    if n >= 2:
                        dve.wait_ge(diff_lo_ready, n - 1)
                    after(window(nc.vector, g, after))
                nc.vector.scalar_tensor_tensor(d[:, w - 1:TP], total[:, NHIST + w - 1:NHIST + TP], 1.0 / w,
                                               u[:, NHIST + w - 1:NHIST + TP], mult, sub)
                nc.vector.scalar_tensor_tensor(d[:, TP:T], total[:, U_S:U_S + TS], 1.0 / w,
                                               u[:, U_S:U_S + TS], mult, sub)
                c = slice(NHIST, NHIST + w - 1)
                after(nc.vector.tensor_tensor(d[:, 0:w - 1], total[:, c], early_count[:, 0:w - 1], mult))
                nc.vector.tensor_tensor(d[:, 0:w - 1], d[:, 0:w - 1], u[:, c], sub).then_inc(diff_ready, 1)

            def mixed_low(n):
                dve.wait_ge(diff_hi_ready, n + 1)
                minus(diff_lo[:, n % 2, :], diff[:, n % 2, :], f32(diff_hi[:, n % 2, :])).then_inc(diff_lo_ready, 1)

            def pool_result(n):
                g = U_ORDER[n]
                dve.wait_ge(pool_hi_ready, n + 1)
                scaled_minus(by_half(b_lo[:, g, :]), halves(ACC[n % 2]), pool_scale[:, g:g + 1],
                             by_half(f32(b_hi[:, g, :]))).then_inc(acc_free, 1)

            mix(0)
            mixed_low(0)
            mix(1)
            mixed_low(1)
            dve.wait_ge(wp_hi_ready, 1)
            minus(wp_lo[:], wp_raw[:], f32(wp_hi[:])).then_inc(wp_ready, 1)
            finish_u(2, 0)
            dve.wait_ge(acc_free, A_U + 3)
            mix(2)
            rest_of_weights(dve, W_O, 0)
            finish_u(3, 1)
            dve.wait_ge(acc_free, A_U + 4)
            mix(3)
            mixed_low(2)
            pool_result(0)
            mixed_low(3)
            pool_result(1)
            take_turns(dve, nc.vector.tensor_copy, 1, EARLY)
            pool_result(2)
            pool_result(3)
            rest_of_weights(dve, W_O + 1, 1)
            take_turns(dve, nc.vector.tensor_copy, 1, MIDDLE)
            take_turns(dve, nc.vector.tensor_copy, 1, LATE)
            for q in range(4):
                n = len(MISCS) - 4 + q
                dve.wait_ge(misc_taken[0], taken(0, n))
                for c in range(2):
                    k = 2 * q + c
                    ins = scaled_minus(mem_lo[:, k, :], MISC[n % 4][:, c * MEM:c * MEM + MEM], g_mkv[:, k:k + 1],
                                       f32(mem_hi[:, k, :]))
                ins.then_inc(mem_gained, 1)


            def flat(x, k):
                return x[:, bass.ds(k, 1), :].rearrange("p k t -> p (k t)")

            def residual_steps(w0, first, gain, lo, hi):
                nc.vector.memset(square_sum[:], 0.0).then_inc(sum_ready, 1)
                with dve.Fori(0, KT // 2) as i:
                    for c in range(2):
                        k = i * 2 + c
                        rest_of_weights(dve, k + (w0 + 2), c)
                        dve.wait_ge(weight_used, k + (w0 + 1))
                        x = flat(x_t, k)
                        nc.vector.tensor_tensor(by_half(x), by_half(x), halves(ACC[c]), add).then_inc(acc_free, 1)
                        dve.wait_ge(acc_free, k + ((A_O if first == 0 else A_MO) + 1))
                        nc.vector.tensor_tensor(gained[:], x, gain[:, bass.ds(k, 1)].to_broadcast([P, T]),
                                                mult).then_inc(gained_ready, 1)
                        dve.wait_ge(act_hi_ready, k + (first + 1))
                        minus(flat(lo, k), gained[:], f32(flat(hi, k)))
                        dve.wait_ge(squared, k + (first + 1))
                        nc.vector.tensor_tensor(square_sum[:], square_sum[:], squares[:], add).then_inc(sum_ready, 1)

            def root(n):
                dve.wait_ge(root_done, n)
                nc.vector.reciprocal(inv_rms[:], inv_rms[:]).then_inc(rms_ready, 1)

            for w in range(2):
                dve.wait_ge(misc_taken[w], taken(w, len(MISCS) - 1))
            residual_steps(W_O, 0, g_xq, a_lo, a_hi)
            with dve.Fori(0, KT // 2) as i:
                for c in range(2):
                    rest_of_weights(dve, i * 2 + (W_MK + 2 + c), c)
            dve.wait_ge(mem_stat_act, 1)
            nc.vector.reciprocal(stat[:, 20:22], stat[:, 18:20]).then_inc(mem_stat_dve, 1)
            root(1)
            dve.wait_ge(rms_ready, 1)
            with dve.Fori(0, KT // 2) as i:
                for c in range(2):
                    k = i * 2 + c
                    rest_of_weights(dve, k + (W_MQ + 2), c)
                    dve.wait_ge(weight_used, k + (W_MQ + 1))
                    dve.wait_ge(mq_ready, k)
                    nc.vector.tensor_tensor(by_half(gained[:]), halves(ACC[c]), by_half(inv_rms[:]), mult).then_inc(acc_free, 1)
                    dve.wait_ge(mq_hi, k + 1)
                    scaled_minus(flat(b_lo, k), gained[:], MSCALE, f32(flat(b_hi, k))).then_inc(mq_ready, 1)

            def memory_keys(s):
                for q in range(4):
                    dve.wait_ge(mk_hi_done, 4 * s + q + 1)
                    k = slice(2 * q, 2 * q + 2)
                    minus(mk_lo[:, s, k, :], ACC[q // 2][:, q % 2].rearrange("p (k m) -> p k m", k=2),
                          f32(mk_hi[:, s, k, :])).then_inc(mk_ready, 1)

            def maxima(s):
                r = P if s < MH else TS
                dve.wait_ge(ms_done, s + 1)
                after(nc.vector.tensor_reduce(stat[0:r, 24:28], memory_scores(s)[0:r].rearrange("p b (q m) -> p (b q) m", q=2), X, ALU.max))
                nc.vector.tensor_scalar(stat[0:r, 28:32], stat[0:r, 24:28], -1.0, None, mult).then_inc(ms_max, 1)

            def normalise(s):
                r = P if s < MH else TS
                dve.wait_ge(ms_exp, s + 1)
                after(nc.vector.reciprocal(stat[0:r, 36:40], stat[0:r, 32:36]))
                for q in range(4):
                    ins = nc.vector.tensor_scalar(mp[0:r, s % 2, q, :], mp[0:r, s % 2, q, :],
                                                  stat[0:r, 36 + q:37 + q], None, mult)
                ins.then_inc(ms_prob, 1)

            for k in range(KT):
                rest_of_weights(dve, W_MV + 2 + k, k % 2)
                if k in (0, 3):
                    memory_keys(k // 3)
                if k == 5:
                    maxima(0)
                    normalise(0)
            dve.wait_ge(kv_hi, 1)
            minus(mv_lo[:, 0], kv_tok[:], f32(mv_hi[:, 0])).then_inc(kv_lo, 1)


            for s in range(MH + 1 + 2):
                if 1 <= s <= MH:
                    maxima(s)
                if s >= 2:
                    m = s - 2
                    dve.wait_ge(mo_hi, m + 1)
                    minus(memory_output(a_lo, m), memory_bank(m), f32(memory_output(a_hi, m))).then_inc(mo_ready, 1)
                if 1 <= s <= MH + 1:
                    m = s - 1
                    w = TP if m < MH else MH * TS
                    dve.wait_ge(mt_hi, m + 1)
                    minus(mpt_lo[:, :, 0:w], OB[:, :, 0:w], f32(mpt_hi[:, :, 0:w])).then_inc(mt_ready, 1)
                if 1 <= s <= MH:
                    normalise(s)

            residual_steps(W_MO, KT, g_ffn, b_lo, b_hi)
            nc.vector.memset(gate[:, 0:2], 0.0)
            nc.vector.memset(hidden[:], 0.0).then_inc(hidden_free, 1)
            root(2)
            dve.wait_ge(rms_ready, 2)
            for k, (f0, nf) in enumerate(CHUNKS):
                with dve.Fori(0, nf) as i:
                    f = i + f0
                    fc = bass.ds(f, 1)
                    rest_of_weights(dve, i * 2 + (W_UP[k] + 2), 0)
                    dve.wait_ge(weight_used, i * 2 + (W_UP[k] + 1))
                    acc = ACC[0]
                    nc.vector.tensor_tensor(gate[:, 2:2 + H], acc[:, 0, 0:H], inv_rms[:, 0:H], mult)
                    nc.vector.tensor_tensor(gate[:, 2 + H:2 + TP], acc[:, 1, 0:TP - H], inv_rms[:, H:TP], mult)
                    nc.vector.tensor_tensor(gate[:, GAP + 2:TE], acc[:, 1, TP - H:H], inv_rms[:, TP:T], mult).then_inc(acc_free, 1)
                    nc.vector.tensor_copy(gate[:, GAP:GAP + 2], conv_hist[:, :, fc].rearrange("p s f -> p (s f)"))
                    nc.vector.tensor_copy(par[:, 0:4], conv_par[:, :, fc].rearrange("p s f -> p (s f)")).then_inc(gate_ready, 1)
                    dve.wait_ge(gate_ready, i + (f0 + 1))
                    dve.wait_ge(acc_free, i * 2 + (A_UP[k] + 1))
                    for g in range(2):
                        c = (TP, TE - 2)[g]
                        nc.vector.tensor_copy(a_last[:, 2 * g:2 * g + 2, fc].rearrange("p s f -> p (s f)"), gate[:, c:c + 2])
                    dve.wait_ge(conv_first, i + (f0 + 1))
                    nc.vector.scalar_tensor_tensor(conv_b[:, 2:TE], gate[:, 1:TE - 1], par[:, 1:2], conv_a[:, 2:TE],
                                                   mult, add).then_inc(conv_second, 1)
                    dve.wait_ge(conv_second, i + (f0 + 1))
                    nc.vector.scalar_tensor_tensor(conv_a[:, 2:TE], gate[:, 0:TE - 2], par[:, 0:1], conv_b[:, 2:TE],
                                                   mult, add).then_inc(conv_ready, 1)
                    dve.wait_ge(weight_used, i * 2 + (W_UP[k] + 2))
                    nc.vector.tensor_tensor(by_half(up_b[:]), halves(ACC[1]), by_half(inv_rms[:]), mult).then_inc(acc_free, 1)
                    dve.wait_ge(acc_free, i * 2 + (A_UP[k] + 2))
                    dve.wait_ge(silu_ready, f + 1)
                    nc.vector.tensor_tensor(hidden[:, 0:TP], silu[:, 0:TP], up_b[:, 0:TP], mult)
                    nc.vector.tensor_tensor(hidden[:, TP:T], silu[:, GAP:GAP + TS], up_b[:, TP:T], mult).then_inc(hidden_ready, 1)
                    dve.wait_ge(hidden_hi, f + 1)
                    minus(flat(a_lo, i), hidden[:], f32(flat(a_hi, i))).then_inc(hidden_free, 1)
                    rest_of_weights(dve, i * 2 + (W_UP[k] + 3), 1)

                def down(k_, n, c):
                    dve.wait_ge(weight_used, n + 1)
                    x = flat(x_t, k_)
                    nc.vector.tensor_tensor(by_half(x), by_half(x), halves(ACC[c]), add).then_inc(acc_free, 1)

                whole = KT // 2 - (k == 2)
                with dve.Fori(0, whole) as i:
                    for c in range(2):
                        rest_of_weights(dve, i * 2 + (W_DOWN[k] + 2 + c), c)
                        down(i * 2 + c, i * 2 + (W_DOWN[k] + c), c)
                if k == 2:
                    for c in range(2):
                        down(KT - 2 + c, W_DOWN[k] + KT - 2 + c, c)
            dve.wait_ge(g_final_landed, 16)
            for t in range(NT + 1):
                r = P if t < NT else TS
                dve.wait_ge(y_root, t + 1)
                after(nc.vector.reciprocal(stat[0:r, 56 + t:57 + t], stat[0:r, 48 + t:49 + t]))
                nc.vector.scalar_tensor_tensor(y_tok[0:r, t, :].rearrange("p (b c) -> p b c", b=2), final_bank(t)[0:r],
                                               stat[0:r, 56 + t:57 + t], g_final[0:r, :].rearrange("p (b c) -> p b c", b=2),
                                               mult, mult).then_inc(y_ready, 1)

        @block.tensor
        def _(pe):
            mm, turn = nc.tensor.matmul, nc.tensor.transpose
            pe.wait_ge(early_ready, 3)
            pe.wait_ge(g_mix_landed, 16)
            bank = OB[:, 1]
            turn(bank[:, 0:KT], rows_in[0:KT, 0, :], ident[0:KT, 0:KT]).then_inc(cols_turned, 1)
            pe.wait_ge(xr_ready, 1)
            for k in range(KT):
                ins = turn(SC[:, 0][:, k * TS:k * TS + TS], xr_tok[0:TS, NT, k * P:k * P + P], ident[0:TS, 0:TS])
            ins.then_inc(hs_turned, 1)
            pe.wait_ge(xr_ready, NT + 1)

            def h_turn(k):
                if k >= 2:
                    pe.wait_ge(h_lo_ready, k - 1)
                b = (SC[:, 1], OB[:, 0])[k % 2]
                for t in range(NT):
                    ins = turn(b[:, t * P:t * P + P], xr_tok[:, t, k * P:k * P + P], ident[:])
                ins.then_inc(h_turned, 1)

            def values(k):
                n, sub = W_V + k // 2, k % 2
                pe.wait_ge(weight_lo_ready, n + 1)
                pe.wait_ge(h_lo_ready, min(k + 2, KT))
                pe.wait_ge(hs_lo_ready, 1)
                c = slice(sub * DFOX, sub * DFOX + DFOX)
                for t in range(NT + 1):
                    b = ACC[t // 2][:, t % 2] if t < NT else SC[:, 0]
                    for x, w in ((0, w_hi), (0, w_lo), (1, w_hi)):
                        ins = mm(b, flat_a[x][:, k * T + t * P:k * T + t * P + P], w[n % 2][:, c],
                                 start=(k == 0 and x == 0 and w is w_hi), stop=(k == KT - 1 and x == 1))
                if sub == 1:
                    ins.then_inc(weight_used, 1)

            h_turn(0)
            h_turn(1)
            pe.wait_ge(rows_landed, 16 * 4)
            pe.wait_ge(more_rows_landed, 16 * 4)
            pe.wait_ge(cols_ready, 1)
            turn(bank[:, 0:NG], rows_in[0:NG, 0, :], ident[0:NG, 0:NG])
            turn(bank[:, 64:64 + 4 * NF], rows_in[0:4 * NF, 1, :], ident[0:4 * NF, 0:4 * NF])
            turn(bank[:, 192:192 + 2 * NF], rows_in[0:2 * NF, 2, :], ident[0:2 * NF, 0:2 * NF])
            for g in range(GROUPS):
                ins = turn(bank[:, 256 + 16 * g:256 + 16 * g + NHIST], hist_tok[0:NHIST, g * P:g * P + P],
                           ident[0:NHIST, 0:NHIST])
            ins.then_inc(cols_turned, 1)
            pe.wait_ge(consts_ready, 10)
            for k in range(KT):
                if k + 2 < KT:
                    h_turn(k + 2)
                values(k)
            pe.wait_ge(wf_ready, 1)
            pe.wait_ge(cols_ready, 4)
            pe.wait_ge(h_lo_ready, KT)
            for k in range(KT):
                for w, x in ((wf_hi, a_hi), (wf_hi, a_lo), (wf_lo, a_hi)):
                    for h in range(2):
                        ins = mm(OB[:, h, 0:H], w[:, k, :], x[:, k, h * H:h * H + H],
                                 start=(k == 0 and w is wf_hi and x is a_hi), stop=(k == KT - 1 and w is wf_lo))
            ins.then_inc(gate_done, 1)
            pe.wait_ge(v_copied, NT + 1)
            pe.wait_ge(v_free, NT + 1)
            for c in range(CT):
                ins = turn(SC[0:HEADS, c // 4, c % 4 * P:c % 4 * P + P], cl_tok[:, c, :], ident[:])
            ins.then_inc(gate_done, 1)

            for n in (W_QK, W_QK + 1):
                pe.wait_ge(weight_lo_ready, n + 1)
                project(n % 2, a_hi, a_lo, ACC[n % 2], range(KT), KT)

            for s in range(STEPS):
                j, e = divmod(s, ENTRIES)
                if s < N_ENTRIES:
                    b = j % 2
                    if s >= 2:
                        pe.wait_ge(scores_taken, s - 1)
                    else:
                        pe.wait_ge(gate_dve, 3)
                    if e == 0:
                        pe.wait_ge(acc_free, A_QK + 2 * j + 2)
                        pe.wait_ge(masks_split, 4)
                    bank, w = SC[:, s % 2], keys_of(e)
                    if e < 2 * NT:
                        h, t = e // NT, e % NT
                        r, c = slice(h * DH, h * DH + DH), slice(t * P, t * P + P)
                        for q, kk in ((q_hi, k_hi), (q_hi, k_lo), (q_lo, k_hi)):
                            mm(bank[:, 0:w], q[r, b, c], kk[r, b, 0:w], start=(q is q_hi and kk is k_hi), stop=False)
                        ins = mm(bank[:, c], ident_r[:], causal_r[:], start=False, stop=True)
                    elif e < ENTRIES - 1:
                        c = slice((e - 2 * NT) * 512, (e - 2 * NT) * 512 + 512)
                        pe.wait_ge(turn_ready, TURN[("K", j, 1)] + 1)
                        for q, kk in ((qs_hi, kc_hi), (qs_hi, kc_lo), (qs_lo, kc_hi)):
                            ins = mm(bank, q[:, b, :], kk[:, c], start=(q is qs_hi and kk is kc_hi), stop=(q is qs_lo))
                    else:
                        for q, kk in ((qs_hi, k_hi), (qs_hi, k_lo), (qs_lo, k_hi)):
                            mm(bank[:, 0:TS], q[:, b, :], kk[:, b, TP:T], start=(q is qs_hi and kk is k_hi), stop=False)
                        ins = mm(bank[:, 0:TS], ident_r[:], causal_s[:], start=False, stop=True)
                    ins.then_inc(scores_done, 1)
                if j < PAIRS and e in FILL:
                    which, tiles = FILL[e]
                    n = W_QK + 2 * (j + 1) + which
                    if tiles[0] == 0:
                        pe.wait_ge(weight_lo_ready, n + 1)
                        pe.wait_ge(acc_free, A_QK + 2 * (j + 1) + which)
                    project(n % 2, a_hi, a_lo, ACC[0], tiles, KT)
                for t in turns_of(s):
                    what = TURNS[t]
                    if t >= 2:
                        pe.wait_ge(turn_ready, t - 1)
                    if what[0] == "K":
                        pe.wait_ge(cache_k_landed, 16 * (what[1] + 1))
                        for c in range(4):
                            ins = turn(TB[t % 2][:, c * P:c * P + P], kc_raw[:, what[2] * 4 + c, :], ident[:])
                    else:
                        e_t = what[1] % ENTRIES
                        pe.wait_ge(prob_ready, probs_done(what[1]))
                        if e_t < 2 * NT:
                            p = prob_p[:, prompt_slot(what[1]), :]
                            n_t = e_t % NT + 1
                        else:
                            p = prob_s[:, (e_t - 2 * NT) * 512:]
                            n_t = 4 if e_t < ENTRIES - 1 else 0
                        for c in range(n_t):
                            ins = turn(TB[t % 2][:, c * P:c * P + P], p[:, c * P:c * P + P], ident[:])
                        if n_t == 0:
                            ins = turn(TB[t % 2][0:TS, 0:P], p[:, 0:TS], ident[:])
                    ins.then_inc(turn_done, 1)
                g = s - LAG - 1
                if 0 <= g < N_ENTRIES:
                    jg, eg = divmod(g, ENTRIES)
                    t = TURN[("P", g)]
                    n, bank = output_of(g)
                    pe.wait_ge(turn_ready, t + 1)
                    if eg % NT == 0 and output_bank_free(n) is not None:
                        pe.wait_ge(o_free, output_bank_free(n))
                    feats = slice(jg * P, jg * P + P)
                    if eg < 2 * NT:
                        out = bank[:, eg % NT * P:eg % NT * P + P]
                        n_k, n_0, n_all = eg % NT + 1, 0, eg % NT + 1
                    else:
                        out = bank[:, 0:P]
                        n_k, n_0, n_all = (4 if eg < ENTRIES - 1 else 1), 4 * (eg - 2 * NT), CT + 1
                        pe.wait_ge(vc_ready, jg + 1)
                    for c in range(n_k):
                        at_c = n_0 + c
                        for vx, px in ((0, pt_hi), (0, pt_lo), (1, pt_hi)):
                            if eg < 2 * NT:
                                v, pp = (v_hi, v_lo)[vx][:, c, feats], px[:, t % 2, c * P:c * P + P]
                            elif eg < ENTRIES - 1:
                                v, pp = (vc_hi, vc_lo)[vx][:, at_c, :], px[:, t % 2, c * P:c * P + P]
                            else:
                                v, pp = (own_hi, own_lo)[vx][:, feats], px[0:TS, t % 2, 0:P]
                            ins = mm(out, v, pp, start=(at_c == 0 and vx == 0 and px is pt_hi),
                                     stop=(at_c == n_all - 1 and vx == 1))
                    ins.then_inc(pv_done, 1)
            for n in (2, 3):
                pe.wait_ge(weight_lo_ready, W_U + n + 1)
                pe.wait_ge(acc_free, A_U + 2)
                pe.wait_ge(turn_ready, len(TURNS))
                project(n % 2, a_hi, a_lo, ACC[n % 2], range(KT), KT)
            pe.wait_ge(wp_ready, 1)
            def pool_map(n):
                g = U_ORDER[n]
                pe.wait_ge(diff_lo_ready, n + 1)
                pe.wait_ge(acc_free, (A_U + 3, A_U + 4, A_U + 5, A_U + 6)[n])
                for w, x in ((wp_hi, diff_hi), (wp_hi, diff_lo), (wp_lo, diff_hi)):
                    for h in range(2):
                        ins = mm(ACC[n % 2][:, h, 0:H], w[:, g, :], x[:, n % 2, h * H:h * H + H],
                                 start=(w is wp_hi and x is diff_hi), stop=(w is wp_lo))
                ins.then_inc(pool_done, 1)

            def misc_turn(n):
                kind, m = MISCS[n]
                bank = MISC[n % 4]
                if n >= 4:
                    w = who(n - 4)
                    pe.wait_ge(misc_taken[w], taken(w, n - 4))
                if kind == "k":
                    r = P if m < NT else TS
                    for j in range(PAIRS):
                        ins = turn(bank[0:r, j * P:j * P + P], k_new[:, j, m * P:m * P + r], ident[:])
                elif kind == "u":
                    end = (NHIST + TP, U_S + TS)[m]
                    for g in range(GROUPS):
                        ins = turn(bank[0:NHIST, g * P:g * P + P], u_all[:, g, end - NHIST:end], ident[:])
                elif kind == "f":
                    for t in range(NT + 1):
                        r = P if t < NT else TS
                        ins = turn(bank[0:r, t * HEADS:t * HEADS + HEADS], logf[:, t * P:t * P + r], ident[0:HEADS, 0:HEADS])
                elif kind == "x":
                    pe.wait_ge(misc_landed, 16 * (NT + 1))
                    for t in range(NT):
                        ins = turn(bank[:, t * P:t * P + P], x_again[:, t, m * P:m * P + P], ident[:])
                elif kind == "xs":
                    for k in range(KT):
                        ins = turn(bank[:, k * TS:k * TS + TS], x_again[0:TS, NT, k * P:k * P + P], ident[0:TS, 0:TS])
                else:
                    pe.wait_ge(mem_landed, 16)
                    for c in range(2):
                        for t in range(MT):
                            ins = turn(bank[:, c * MEM + t * P:c * MEM + t * P + P],
                                       mem_tok[:, t, (2 * m + c) * P:(2 * m + c) * P + P], ident[:])
                ins.then_inc(misc_turned, 1)

            pool_map(0)
            pool_map(1)
            pe.wait_ge(scores_taken, N_ENTRIES)
            pe.wait_ge(o_free, OUTPUTS * PAIRS)
            for n in EARLY:
                misc_turn(n)
            pool_map(2)
            pool_map(3)
            for n in MIDDLE:
                misc_turn(n)

            def mean(n, value, bank):
                pe.wait_ge(sum_ready, value)
                for h in range(2):
                    ins = mm(bank[:, h, 0:H], mean_w[:], square_sum[:, h * H:h * H + H], start=True, stop=True)
                ins.then_inc(mean_done, 1)

            def project_all(w0, a0, x_hi, x_lo, total=KT, rounds=KT // 2, ready=None, second=None):
                with pe.Fori(0, rounds) as i:
                    for c in range(2):
                        pe.wait_ge(weight_lo_ready, i * 2 + (w0 + c + 1))
                        pe.wait_ge(acc_free, i * 2 + (a0 + c - 1))
                        if c == 1 and second is not None:
                            pe.wait_ge(*second)
                        project(c, x_hi, x_lo, ACC[c], range(total), total, ready)

            pe.wait_ge(acc_free, A_O)
            for c in range(2):
                pe.wait_ge(weight_lo_ready, W_O + c + 1)
                project(c, b_hi, b_lo, ACC[c], range(KT), KT)
                if c == 0:
                    for n in LATE:
                        misc_turn(n)
            project_all(W_O + 2, A_O + 2, b_hi, b_lo, rounds=KT // 2 - 1)

            def memory_tile(n, slot, k, first, last):
                pe.wait_ge(weight_lo_ready, n + 1)
                for t in range(MT):
                    for h in range(2):
                        for x, w in ((mem_hi, w_hi), (mem_lo, w_hi), (mem_hi, w_lo)):
                            ins = mm((SC, OB)[t][:, h], x[:, k, t * P:t * P + P], w[slot][:, h * 512:h * 512 + 512],
                                     start=(first and x is mem_hi and w is w_hi), stop=(last and w is w_lo))
                ins.then_inc(weight_used, 1)

            pe.wait_ge(mem_gained, 4)
            for k in range(KT // 2):
                memory_tile(W_MK + k, k % 2, k, k == 0, False)
            pe.wait_ge(acc_free, A_O + KT)
            mean(1, KT + 1, ACC[1])
            for k in range(KT // 2, KT):
                memory_tile(W_MK + k, k % 2, k, False, k == KT - 1)
            project_all(W_MQ, A_MQ, a_hi, a_lo, second=(root_done, 1))

            def memory_keys(s):
                pe.wait_ge(acc_free, A_MQ + KT)
                if s == 0:
                    pe.wait_ge(kv_out, 2)
                else:
                    pe.wait_ge(ck_landed, 16)
                    pe.wait_ge(mk_ready, 4)
                for q in range(4):
                    for c in range(2):
                        for t in range(MT):
                            ins = turn(ACC[q // 2][:, q % 2, c * MEM + t * P:c * MEM + t * P + P],
                                       kv_tok[:, t, (2 * q + c) * P:(2 * q + c) * P + P], ident[:])
                    ins.then_inc(mk_turned, 1)

            def scores(s):
                for q in range(4):
                    out = memory_scores(s)[:, q // 2, q % 2 * MEM:q % 2 * MEM + MEM]
                    for f in range(2):
                        k = 2 * (s if s < MH else q) + f
                        col = k * T + (q * P if s < MH else TP)
                        for x, kk in ((0, mk_hi), (0, mk_lo), (1, mk_hi)):
                            ins = mm(out, flat_b[x][:, col:col + P], kk[:, s // MH, k, :],
                                     start=(f == 0 and x == 0 and kk is mk_hi), stop=(f == 1 and x == 1))
                ins.then_inc(ms_done, 1)

            pe.wait_ge(kv_out, 2)
            for k in range(KT):
                memory_tile(W_MV + k, k % 2, k, k == 0, k == KT - 1)
                if k in (0, 3):
                    memory_keys(k // 3)
                if k == 5:
                    pe.wait_ge(mq_ready, KT)
                    pe.wait_ge(mk_ready, 8)
                    scores(0)

            for s in range(MH + 1 + 2):
                if 1 <= s <= MH:
                    if s >= 2:
                        pe.wait_ge(ms_exp, s - 1)
                    if s == 1:
                        pe.wait_ge(kv_out, 4)
                    scores(s)
                if s >= 2:
                    m = s - 2
                    pe.wait_ge(mt_ready, m + 1)
                    if m < MH:
                        pe.wait_ge(kv_lo, 1)
                    else:
                        pe.wait_ge(cached_lo, MT)
                    if m >= 1:
                        pe.wait_ge(mo_ready, m)
                    for f in range(2 if m < MH else 2 * MH):
                        if m < MH:
                            out, c, k = ACC[0][:, f], slice(0, TP), 2 * m + f
                        else:
                            out, k = ACC[0][:, 0, f * TS:f * TS + TS], f
                            c = slice(f // 2 * TS, f // 2 * TS + TS)
                        for b in range(MT):
                            for v, pp in ((mv_hi, mpt_hi), (mv_hi, mpt_lo), (mv_lo, mpt_hi)):
                                ins = mm(out, v[:, m // MH, b, k * P:k * P + P], pp[:, b, c],
                                         start=(b == 0 and v is mv_hi and pp is mpt_hi), stop=(b == MT - 1 and v is mv_lo))
                    ins.then_inc(mo_done, 1)
                if 1 <= s <= MH + 1:
                    m = s - 1
                    pe.wait_ge(ms_prob, m + 1)
                    if m >= 1:
                        pe.wait_ge(mt_ready, m)
                    for b in range(MT):
                        for q in range(4):
                            if m < MH:
                                ins = turn(OB[:, b, q * P:q * P + P], mp[:, m % 2, q, b * P:b * P + P], ident[:])
                            else:
                                ins = turn(OB[:, b, q * TS:q * TS + TS], mp[0:TS, m % 2, q, b * P:b * P + P], ident[0:TS, 0:TS])
                    ins.then_inc(mt_done, 1)
            pe.wait_ge(mo_ready, MH + 1)
            project_all(W_MO, A_MO, a_hi, a_lo)
            for c in range(2):
                pe.wait_ge(weight_lo_ready, W_UP[0] + c + 1)
                pe.wait_ge(acc_free, A_UP[0] + c - 1)
                for f in range(KT):
                    if c == 0:
                        pe.wait_ge(sum_ready, KT + 2 + f + 1)
                    project(c, b_hi, b_lo, ACC[c], [f], KT)
                if c == 0:
                    mean(2, 2 * KT + 2, SC)
            for k, (f0, nf) in enumerate(CHUNKS):
                project_all(W_UP[k] + 2 * (k == 0), A_UP[k] + 2 * (k == 0), b_hi, b_lo, rounds=nf - (k == 0))
                pe.wait_ge(hidden_free, f0 + nf)
                project_all(W_DOWN[k], A_DOWN[k], a_hi, a_lo, total=nf, ready=(hidden_free, f0 + nf + 1))
            turn(MISC[0][0:4 * NF, 0:P], a_last[:].rearrange("p s f -> p (s f)"), ident[:]).then_inc(conv_turned, 1)
            pe.wait_ge(acc_free, a_all)
            for t in range(NT + 1):
                r = P if t < NT else TS
                if t == 1:
                    pe.wait_ge(conv_tok_ready, 1)
                if t == NT:
                    pe.wait_ge(y_ready, 1)
                for k in range(KT):
                    ins = turn(final_bank(t)[0:r, k // 4, k % 4 * P:k % 4 * P + P], x_t[:, k, t * P:t * P + r], ident[:])
                ins.then_inc(y_turned, 1)


_INS = ['x_prompt', 'x_sample', 'cache_fox_k', 'cache_fox_v', 'cache_fox_logf', 'state_pool', 'state_ffn_conv',
        'cache_mem_k', 'cache_mem_v', 'mem_prompt', 'g_mix', 'w_in', 'b_f', 'w_pool', 'pool_scale', 'w_o',
        'g_xq', 'g_mkv', 'w_mq', 'w_mk', 'w_mv', 'w_mo', 'g_ffn', 'w_up', 'conv_w', 'conv_b', 'w_down', 'g_final']


def declare(nc, shapes):
    a = {n: nc.dram_tensor(f"in_{n}", shapes[n], F32, kind="ExternalInput").ap() for n in _INS}
    depth, batch, past, heads, dh = shapes['cache_fox_k']
    _, tp, d = shapes['x_prompt']
    ts = shapes['x_sample'][1]
    mem = shapes['cache_mem_k'][2:]
    outs = [('y_prompt', (batch, tp, d)), ('y_sample', (batch, ts, d)),
            ('fox_k_prompt', (depth, batch, tp, heads, dh)), ('fox_v_prompt', (depth, batch, tp, heads, dh)),
            ('fox_logf_prompt', (depth, batch, tp, heads)), ('pool_state_prompt', shapes['state_pool']),
            ('conv_state_prompt', shapes['state_ffn_conv']), ('mem_k_prompt', (depth, batch) + tuple(mem)),
            ('mem_v_prompt', (depth, batch) + tuple(mem)),
            ('fox_k_sample', (depth, batch, ts, heads, dh)), ('fox_v_sample', (depth, batch, ts, heads, dh)),
            ('fox_logf_sample', (depth, batch, ts, heads)), ('pool_state_sample', shapes['state_pool']),
            ('conv_state_sample', shapes['state_ffn_conv'])]
    o = {n: nc.dram_tensor(f"out_{n}", s, F32, kind="ExternalOutput").ap() for n, s in outs}
    build(nc, a, o)
    return [n for n, _ in outs]


def kernel(**inputs):
    import concourse.bacc as bacc
    import numpy as np
    from concourse.bass_utils import run_bass_kernel_spmd as run

    arrays = {n: np.ascontiguousarray(inputs[n]) for n in _INS}
    nc = bacc.Bacc("TRN2", target_bir_lowering=False, num_devices=1, dynamic_dma_scratch_size=DMA_SCRATCH)
    names = declare(nc, {n: x.shape for n, x in arrays.items()})
    r = run(nc, [{f"in_{n}": x for n, x in arrays.items()}], core_ids=[0])
    return tuple(r.results[0][f"out_{n}"] for n in names)
```
